# Optimizing a Trainium2 kernel written in Bass

```python
import numpy as np
import jax, jax.numpy as jnp
from jax import lax

D_MODEL = 1024
BATCH = 1
SEQ = 512
DEPTH = 2

CHUNK = 64
HEAD_DIM = 64
ATTN_HEADS = 8
ATTN_KV_HEADS = 2
ATTN_GROUP = ATTN_HEADS // ATTN_KV_HEADS
WINDOW = 128
WINDOW_CHUNKS = WINDOW // CHUNK
HGRN_HEADS = 8
HGRN_K = 64
HGRN_V = 64
ATTN_WIDTH = ATTN_HEADS * HEAD_DIM
ATTN_KV_WIDTH = ATTN_KV_HEADS * HEAD_DIM
HGRN_KW = HGRN_HEADS * HGRN_K
HGRN_WIDTH = HGRN_HEADS * HGRN_V
MIX_WIDTH = ATTN_WIDTH + HGRN_WIDTH
IN_COLS = ATTN_WIDTH + 2 * ATTN_KV_WIDTH + 2 * HGRN_KW + 2 * HGRN_WIDTH
D_FF = 2816
REL_BUCKETS = 32
REL_MAX_DIST = 128
NORM_EPS = 1e-6
NEG_INF = -1e30

kernel_name = 'hymba_swa_sink_hgrn2_macaron_sandwich'

def rms_norm(x, gain):
    xf = x.astype(jnp.float32)
    y = xf * lax.rsqrt(jnp.mean(xf * xf, axis=-1, keepdims=True) + NORM_EPS)
    return (y * gain.astype(jnp.float32)).astype(x.dtype)

def swiglu(h, w_up, w_down):
    gate, up = jnp.split(h @ w_up, 2, axis=-1)
    return (jax.nn.silu(gate) * up) @ w_down

def t5_bucket(rel):
    nb = REL_BUCKETS // 2
    ret = (rel > 0).astype(np.int32) * nb
    n = np.abs(rel)
    max_exact = nb // 2
    large = max_exact + (np.log(np.maximum(n, 1) / max_exact) / np.log(REL_MAX_DIST / max_exact) * (nb - max_exact)).astype(np.int32)
    large = np.minimum(large, nb - 1)
    return ret + np.where(n < max_exact, n, large)

def sliding_window_sink_attention(q, k, v, sinks, rel_bias):
    b, s = q.shape[0], q.shape[1]
    nc = s // CHUNK
    qb = q.reshape(b, nc, CHUNK, ATTN_KV_HEADS, ATTN_GROUP, HEAD_DIM)

    def band(t):
        t = t.reshape(b, nc, CHUNK, ATTN_KV_HEADS, HEAD_DIM)
        tp = jnp.pad(t, ((0, 0), (WINDOW_CHUNKS - 1, 0), (0, 0), (0, 0), (0, 0)))
        return jnp.concatenate([tp[:, i:i + nc] for i in range(WINDOW_CHUNKS)], axis=2)

    kw, vw = band(k), band(v)
    logits = jnp.einsum('bnqhgd,bnkhd->bnhgqk', qb, kw).astype(jnp.float32) * (HEAD_DIM ** -0.5)
    q_pos = np.arange(CHUNK)[:, None] + (WINDOW_CHUNKS - 1) * CHUNK
    k_pos = np.arange(WINDOW_CHUNKS * CHUNK)[None, :]
    bucket = t5_bucket(k_pos - q_pos)
    bias = jnp.transpose(rel_bias[bucket], (2, 0, 1)).reshape(ATTN_KV_HEADS, ATTN_GROUP, CHUNK, WINDOW_CHUNKS * CHUNK)
    key_chunk = np.arange(nc)[:, None] - (WINDOW_CHUNKS - 1) + k_pos // CHUNK
    valid = key_chunk >= 0
    logits = jnp.where(valid[None, :, None, None, None, :], logits + bias.astype(jnp.float32), NEG_INF)
    sink = sinks.astype(jnp.float32).reshape(ATTN_KV_HEADS, ATTN_GROUP)[None, None, :, :, None, None]
    m = jnp.maximum(jnp.max(logits, axis=-1, keepdims=True), sink)
    p = jnp.exp(logits - m)
    probs = p / (jnp.sum(p, axis=-1, keepdims=True) + jnp.exp(sink - m))
    o = jnp.einsum('bnhgqk,bnkhd->bnqhgd', probs.astype(vw.dtype), vw)
    return o.reshape(b, s, ATTN_WIDTH)

def hgrn2_mixer(q, f, i, gate, lb, norm_gain, first_layer):
    b, s = q.shape[0], q.shape[1]
    nc = s // CHUNK
    qf = jax.nn.silu(q.astype(jnp.float32))
    ff = f.astype(jnp.float32)
    if first_layer:
        log_f = jax.nn.log_sigmoid(ff)
        kf = jax.nn.sigmoid(-ff)
    else:
        lbh = lb.astype(jnp.float32).reshape(HGRN_HEADS, HGRN_K)
        fg = lbh + (1.0 - lbh) * jax.nn.sigmoid(ff)
        log_f = jnp.log(fg)
        kf = 1.0 - fg

    def to_chunks(t, d):
        return t.reshape(b, nc, CHUNK, HGRN_HEADS, d).transpose(1, 0, 3, 2, 4)

    qc, kc, gc = to_chunks(qf, HGRN_K), to_chunks(kf, HGRN_K), to_chunks(log_f, HGRN_K)
    vc = to_chunks(i.astype(jnp.float32), HGRN_V)
    tri = np.tril(np.ones((CHUNK, CHUNK), dtype=bool))[:, :, None]

    def step(state, inp):
        qj, kj, vj, gj = inp
        bcum = jnp.cumsum(gj, axis=2)
        diff = bcum[:, :, :, None, :] - bcum[:, :, None, :, :]
        decay = jnp.where(tri, jnp.exp(jnp.where(tri, diff, 0.0)), 0.0)
        scores = jnp.einsum('bhjk,bhjik,bhik->bhji', qj, decay, kj)
        o = jnp.einsum('bhji,bhiv->bhjv', scores, vj) + jnp.einsum('bhjk,bhkv->bhjv', qj * jnp.exp(bcum), state)
        blast = bcum[:, :, -1:, :]
        new_state = jnp.exp(blast[:, :, 0, :, None]) * state + jnp.einsum('bhik,bhiv->bhkv', kj * jnp.exp(blast - bcum), vj)
        return new_state, o

    s0 = jnp.zeros((b, HGRN_HEADS, HGRN_K, HGRN_V), jnp.float32)
    _, oc = lax.scan(step, s0, (qc, kc, vc, gc))
    o = oc.transpose(1, 0, 3, 2, 4).reshape(b, s, HGRN_HEADS, HGRN_V)
    o = o * lax.rsqrt(jnp.mean(o * o, axis=-1, keepdims=True) + NORM_EPS)
    o = o * norm_gain.astype(jnp.float32).reshape(HGRN_HEADS, HGRN_V)
    o = o.reshape(b, s, HGRN_WIDTH) * jax.nn.silu(gate.astype(jnp.float32))
    return o.astype(gate.dtype)

def setup_inputs(seed: int = 0) -> dict:
    key = jax.random.key(seed)
    ks = jax.random.split(key, 12)
    f32 = jnp.float32
    x = jax.random.normal(ks[0], (BATCH, SEQ, D_MODEL), f32)
    norm_gains = 1.0 + 0.05 * jax.random.normal(ks[1], (DEPTH, 6, D_MODEL), f32)
    w_ffn_in = jax.random.normal(ks[2], (DEPTH, 2, D_MODEL, 2 * D_FF), f32) * D_MODEL ** -0.5
    w_ffn_out = jax.random.normal(ks[3], (DEPTH, 2, D_FF, D_MODEL), f32) * D_FF ** -0.5
    w_in = jax.random.normal(ks[4], (DEPTH, D_MODEL, IN_COLS), f32) * D_MODEL ** -0.5
    w_out = jax.random.normal(ks[5], (DEPTH, MIX_WIDTH, D_MODEL), f32) * MIX_WIDTH ** -0.5
    attn_sinks = 0.5 * jax.random.normal(ks[6], (DEPTH, ATTN_HEADS), f32)
    attn_out_gain = 1.0 + 0.05 * jax.random.normal(ks[7], (DEPTH, ATTN_WIDTH), f32)
    rel_bias = 0.5 * jax.random.normal(ks[8], (REL_BUCKETS, ATTN_HEADS), f32)
    hgrn_lb_logits = 0.5 * jax.random.normal(ks[9], (DEPTH, HGRN_KW), f32)
    hgrn_norm_gain = 1.0 + 0.05 * jax.random.normal(ks[10], (DEPTH, HGRN_WIDTH), f32)
    return {'x': x, 'norm_gains': norm_gains, 'w_ffn_in': w_ffn_in, 'w_ffn_out': w_ffn_out,
            'w_in': w_in, 'w_out': w_out, 'attn_sinks': attn_sinks, 'attn_out_gain': attn_out_gain,
            'rel_bias': rel_bias, 'hgrn_lb_logits': hgrn_lb_logits, 'hgrn_norm_gain': hgrn_norm_gain}

def reference(x, norm_gains, w_ffn_in, w_ffn_out, w_in, w_out, attn_sinks, attn_out_gain,
              rel_bias, hgrn_lb_logits, hgrn_norm_gain):
    b, s = x.shape[0], x.shape[1]
    lb_probs = jax.nn.softmax(hgrn_lb_logits.astype(jnp.float32), axis=0)
    lower_bounds = jnp.cumsum(lb_probs, axis=0) - lb_probs[0]
    splits = [ATTN_WIDTH, ATTN_WIDTH + ATTN_KV_WIDTH, ATTN_WIDTH + 2 * ATTN_KV_WIDTH,
              ATTN_WIDTH + 2 * ATTN_KV_WIDTH + HGRN_KW, ATTN_WIDTH + 2 * ATTN_KV_WIDTH + 2 * HGRN_KW,
              ATTN_WIDTH + 2 * ATTN_KV_WIDTH + 2 * HGRN_KW + HGRN_WIDTH]
    for layer in range(DEPTH):
        g = norm_gains[layer]
        h = rms_norm(x, g[0])
        x = x + 0.5 * rms_norm(swiglu(h, w_ffn_in[layer, 0], w_ffn_out[layer, 0]), g[1])
        h = rms_norm(x, g[2])
        proj = h @ w_in[layer]
        qa, ka, va, qh, fh, ih, gh = jnp.split(proj, splits, axis=-1)
        ya = sliding_window_sink_attention(
            qa.reshape(b, s, ATTN_HEADS, HEAD_DIM), ka.reshape(b, s, ATTN_KV_HEADS, HEAD_DIM),
            va.reshape(b, s, ATTN_KV_HEADS, HEAD_DIM), attn_sinks[layer], rel_bias)
        ya = rms_norm(ya, attn_out_gain[layer])
        yh = hgrn2_mixer(qh.reshape(b, s, HGRN_HEADS, HGRN_K), fh.reshape(b, s, HGRN_HEADS, HGRN_K),
                         ih.reshape(b, s, HGRN_HEADS, HGRN_V), gh, lower_bounds[layer],
                         hgrn_norm_gain[layer], layer == 0)
        y = jnp.concatenate([ya.astype(x.dtype), yh.astype(x.dtype)], axis=-1) @ w_out[layer]
        x = x + rms_norm(y, g[3])
        h = rms_norm(x, g[4])
        x = x + 0.5 * rms_norm(swiglu(h, w_ffn_in[layer, 1], w_ffn_out[layer, 1]), g[5])
    return x


_drawn_inputs = setup_inputs


def setup_inputs(seed=0):
    import zlib

    import numpy as np

    out = dict(_drawn_inputs(seed))
    spreads = {}
    factors = {'attn_sinks': 8.0}
    for name, (base, spread) in spreads.items():
        noise = np.random.default_rng([zlib.crc32(name.encode()), seed]).standard_normal(out[name].shape)
        drawn = base * np.exp(spread * noise) if base else spread * noise
        out[name] = __import__('jax').numpy.asarray(drawn.astype(out[name].dtype))
    for name, factor in factors.items():
        out[name] = (out[name] * factor).astype(out[name].dtype)
    return out
```

```python
from contextlib import ExitStack

import numpy as np

import concourse.bass as bass
from concourse import mybir
from concourse.alu_op_type import AluOpType as ALU

ACT = mybir.ActivationFunctionType
F32 = mybir.dt.float32
F32R = mybir.dt.float32r
U32 = mybir.dt.uint32
AX_X = mybir.AxisListType.X

P = 128
DEPTH, SEQ, D_MODEL, D_FF = 2, 512, 1024, 2816
HEADS, HEAD_DIM, CHUNK = 8, 64, 64
WINDOW = 2 * CHUNK
KT = D_MODEL // P
FT = D_FF // P
NT = HEADS // 2
BUCKETS, REL_MAX_DIST = 32, 128
NORM_EPS = 1e-6
NEG_INF = -1e30
FG_MIN = 2.0 ** -63

HCHUNKS = SEQ // P
HALVES = [64, 32, 16, 8, 4, 2, 1]
NLEV = len(HALVES)
STAGES = NLEV + 2
RELS = WINDOW + CHUNK - 1

RAW_SLOTS, SPLIT_SLOTS, PROJ_BANKS, SQ_SLOTS = 4, 2, 4, 2
TILES = 8
CW = TILES * P
DOWN_CHUNKS = -(-FT // TILES)
FFN_IN, FFN_OUT = 2 * FT, KT * DOWN_CHUNKS
KV_CHUNKS = 4
C_UP0 = 0
C_DOWN0 = C_UP0 + FFN_IN
C_KV = C_DOWN0 + FFN_OUT
C_GROUP0 = C_KV + KV_CHUNKS
C_GROUPS = C_GROUP0 + 4
C_OUT = C_GROUPS + 4 * NT
C_UP1 = C_OUT + KT
C_DOWN1 = C_UP1 + FFN_IN
LAYER_CHUNKS = C_DOWN1 + FFN_OUT
assert all(c % RAW_SLOTS == 0 for c in (C_DOWN0, C_KV, C_GROUP0, C_OUT, C_UP1, C_DOWN1, LAYER_CHUNKS))

J_UP0 = 0
J_DOWN0 = J_UP0 + FFN_IN
J_KV = J_DOWN0 + KT
J_GROUP0 = J_KV + 2
J_GROUPS = J_GROUP0 + 4
J_OUT = J_GROUPS + 4 * NT
J_UP1 = J_OUT + KT
J_DOWN1 = J_UP1 + FFN_IN
LAYER_JOBS = J_DOWN1 + KT

Q_PRE = [0, 16, 36]
Q_YA = 24
Q_POST = [8, 28, 44]
LAYER_SQ = 52

P_GAIN, P_YA, P_YH, P_SINK, P_LB = 0, 6 * KT, 6 * KT + NT, 6 * KT + 2 * NT, 6 * KT + 3 * NT
P_COLS = P_LB + NT


def t5_bucket_one_hot():
    rel = np.arange(RELS) - (WINDOW - 1)
    nb = BUCKETS // 2
    n, exact = np.abs(rel), nb // 2
    large = exact + (np.log(np.maximum(n, 1) / exact) / np.log(REL_MAX_DIST / exact) * (nb - exact)).astype(np.int32)
    bucket = (rel > 0).astype(np.int32) * nb + np.where(n < exact, n, np.minimum(large, nb - 1))
    return (bucket[None, :] == np.arange(BUCKETS)[:, None]).astype(np.float32)


def level_masks():
    out = np.zeros((P, NLEV, P // 2), np.uint32)
    key = np.arange(P)
    for n, m in enumerate(HALVES):
        for q in range(P // 2):
            out[:, n, q] = (key // (2 * m) == q // m) & (key % (2 * m) < m)
    return out.reshape(P, -1)


def build_program(nc, xT, stream, params, sinks, rel_bias, one_hot, masks, out):
    with ExitStack() as ctx:
        def sb(name, shape, dt=F32, scope=ctx):
            return scope.enter_context(nc.sbuf_tensor(name, shape, dt))

        def sem(name):
            return ctx.enter_context(nc.semaphore(name))

        X = sb("X", [P, KT, SEQ])
        HHI = sb("HHI", [P, KT, SEQ], F32R)
        HLO = sb("HLO", [P, KT, SEQ], F32R)
        RAW = sb("RAW", [P, RAW_SLOTS, CW])
        WHI = sb("WHI", [P, SPLIT_SLOTS, CW], F32R)
        WLO = sb("WLO", [P, SPLIT_SLOTS, CW], F32R)
        Y = sb("Y", [P, KT, SEQ])
        R = sb("R", [P, SEQ])
        RP = sb("RP", [P, SEQ])
        SS = sb("SS", [P, SEQ])
        SQ = sb("SQ", [P, SQ_SLOTS, SEQ])
        TMP = sb("TMP", [P, SEQ])
        UB = sb("UB", [P, SEQ])
        ones = sb("ones", [P, P])
        block_ones = sb("block_ones", [P, P])
        ident = sb("ident", [P, P])
        par = sb("par", [P, DEPTH, P_COLS])
        cur = sb("cur", [P, P_COLS])
        bias = sb("bias", [P, NT, WINDOW])
        level_mask = sb("level_mask", [P, NLEV * (P // 2)], U32)
        eps = sb("eps", [P, 1])
        lbw = sb("lbw", [P, 6, NT])
        lb_all = sb("lb_all", [P, DEPTH, 2 * NT])
        lb = sb("lb", [P, 2 * NT])
        small = sb("small", [P, 3, 8])
        edec = sb("edec", [P, HCHUNKS])

        with ExitStack() as ffn_scope:
            UHI = sb("UHI", [P, FT, SEQ], F32R, ffn_scope)
            ULO = sb("ULO", [P, FT, SEQ], F32R, ffn_scope)
        kT = sb("kT", [P, CHUNK + SEQ])
        vT = sb("vT", [P, CHUNK + SEQ])
        vwin = sb("vwin", [P, 8, P])
        KZ = sb("KZ", [P, NLEV, SEQ])
        QC = sb("QC", [P, NLEV, HCHUNKS, P // 2])
        SM = sb("SM", [P, 2, HCHUNKS, P])
        S = sb("S", [P, 8 * WINDOW + 8])
        PT = sb("PT", [P, 8, P])
        PROJ = sb("PROJ", [P, 4, SEQ])
        GATE = sb("GATE", [P, 4, SEQ])
        BC = sb("BC", [P, SEQ])
        KK = sb("KK", [P, SEQ])
        DD = sb("DD", [P, 4, SEQ])
        QB = sb("QB", [P, SEQ])
        KH = sb("KH", [P, SEQ])
        KHT = sb("KHT", [P, HCHUNKS, P])
        VTOK = sb("VTOK", [P, HCHUNKS, P])
        ST = sb("ST", [P, HCHUNKS - 1, HEAD_DIM])
        G = sb("G", [P, NT, SEQ])
        Slog = S[:, 0:8 * WINDOW].rearrange("p (n k) -> p n k", n=8)
        Ssink = S[:, 8 * WINDOW:]
        SIGF, SIGNF, SIGQ, LF = (GATE[:, n, :] for n in range(4))

        bank = [ctx.enter_context(nc.psum_tensor(f"bank{n}", [P, SEQ], F32)) for n in range(8)]

        rel_scratch = nc.dram_tensor("rel_scratch", (CHUNK * HEADS * RELS,), F32, kind="Internal").ap()
        relT = KZ[0:CHUNK, 0:3, :].rearrange("p a b -> p (a b)")[:, 0:HEADS * RELS]
        oh_sb = QC[0:BUCKETS, 0, :, :].rearrange("p a b -> p (a b)")[:, 0:RELS]
        rel_sb = small[0:BUCKETS, 0, :]
        oh_rel = Y[0:BUCKETS, 0:3, :].rearrange("p a b -> p (a b)")[:, 0:HEADS * RELS]

        w_dma = [sem(f"w_dma{n}") for n in range(RAW_SLOTS)]
        w_hi = sem("w_hi")
        w_split = sem("w_split")
        w_used = sem("w_used")
        proj_free = sem("proj_free")
        sq_done = sem("sq_done")
        sq_free = sem("sq_free")
        start_credit = sem("start_credit")
        const_dma = sem("const_dma")
        const_ready = sem("const_ready")
        setup = sem("setup")
        setup_act = sem("setup_act")
        setup_pe = sem("setup_pe")
        setup_dma = sem("setup_dma")
        cur_ready = sem("cur_ready")
        x_ready = sem("x_ready")
        h_hi = sem("h_hi")
        h_lo = sem("h_lo")
        pre_sum = sem("pre_sum")
        pre_r = sem("pre_r")
        post_sum = sem("post_sum")
        post_r = sem("post_r")
        silu_ready = sem("silu_ready")
        u_ready = sem("u_ready")
        u_hi = sem("u_hi")
        u_lo = sem("u_lo")
        vwin_full = sem("vwin_full")
        vwin_ready = sem("vwin_ready")
        qk_full = sem("qk_full")
        logit_ready = sem("logit_ready")
        exp_ready = sem("exp_ready")
        p_ready = sem("p_ready")
        pt_full = sem("pt_full")
        pt_ready = sem("pt_ready")
        pv_full = sem("pv_full")
        ya_ready = sem("ya_ready")
        sig_ready = sem("sig_ready")
        fg_ready = sem("fg_ready")
        lf_ready = sem("lf_ready")
        bc_ready = sem("bc_ready")
        edec_ready = sem("edec_ready")
        exponent = sem("exponent")
        decay = sem("decay")
        staged = sem("staged")
        vtok_full = sem("vtok_full")
        vtok_ready = sem("vtok_ready")
        kht_full = sem("kht_full")
        kht_ready = sem("kht_ready")
        ds_full = sem("ds_full")
        st_ready = sem("st_ready")
        lv_full = sem("lv_full")
        lv_used = sem("lv_used")
        o_full = sem("o_full")
        o_ready = sem("o_ready")
        g_sig = sem("g_sig")
        ya_sum = sem("ya_sum")
        ya_r = sem("ya_r")
        yh_sq = sem("yh_sq")
        yh_sum = sem("yh_sum")
        yh_r = sem("yh_r")
        z_ready = sem("z_ready")
        z_hi = sem("z_hi")
        z_lo = sem("z_lo")
        stored = sem("stored")
        held = sem("held")

        block = ctx.enter_context(nc.Block())

        @block.sync
        def _(sp):
            sp.dma_start(par[:], params).then_inc(const_dma, 16)
            for half in range(2):
                dst = par[half * 64:half * 64 + 64, :, P_SINK:P_SINK + NT]
                src = sinks[:, half * NT:half * NT + NT].unsqueeze(0).to_broadcast([64, DEPTH, NT])
                sp.wait_ge(const_dma, 16 * (1 + half))
                sp.dma_start(dst, src).then_inc(const_dma, 16)
            sp.dma_start(rel_sb, rel_bias).then_inc(const_dma, 16)
            sp.dma_start(oh_sb, one_hot).then_inc(const_dma, 16)
            sp.dma_start(level_mask[:], masks).then_inc(const_dma, 16)
            sp.dma_start(X[:], xT).then_inc(const_dma, 16)
            for n in range(RAW_SLOTS):
                sp.dma_start(RAW[:, n, :], stream[n]).then_inc(w_dma[n], 16)
            sp.wait_ge(setup, 3)
            sp.dma_start(rel_scratch.rearrange("(q c) -> q c", q=CHUNK), relT).then_inc(setup_dma, 16)
            sp.wait_ge(setup_dma, 16)
            for half in range(2):
                base = half * NT * RELS + CHUNK - 1
                src = bass.AP(tensor=rel_scratch.tensor, offset=base,
                              ap=[[HEADS * RELS - 1, CHUNK], [RELS, NT], [1, WINDOW]])
                sp.dma_start(bias[half * 64:half * 64 + 64, :, :], src).then_inc(setup_dma, 16)
            with sp.Fori(1, DEPTH * LAYER_CHUNKS // RAW_SLOTS) as i:
                for n in range(RAW_SLOTS):
                    sp.wait_ge(w_split, i * RAW_SLOTS + (n + 1))
                    sp.dma_start(RAW[:, n, :], stream[i * RAW_SLOTS + n]).then_inc(w_dma[n], 16)
            for k in range(KT):
                sp.wait_ge(x_ready, 8 * (3 * DEPTH) + k + 1)
                sp.dma_start(out[:, k, :], X[:, k, :]).then_inc(stored, 16)
            sp.wait_ge(stored, 16 * KT)

        @block.gpsimd
        def _(pool):
            pool.memset(eps[:], NORM_EPS)
            pool.memset(ones[:], 1.0)
            pool.memset(block_ones[:], 0.0)
            pool.memset(ident[:], 0.0)
            pool.drain()
            for h in range(2):
                pool.memset(block_ones[64 * h:64 * h + 64, 64 * h:64 * h + 64], 1.0)
                pool.drain()
            pool.affine_select(out=ident[:], in_=ident[:], compare_op=ALU.not_equal, fill=1.0, base=0,
                               pattern=[[-1, P]], channel_multiplier=1)
            pool.drain()
            pool.memset(small[:, 2, 0:1], 0.0).then_inc(w_split, RAW_SLOTS)
            pool.memset(small[:, 2, 1:2], 0.0).then_inc(w_used, SPLIT_SLOTS)
            pool.memset(small[:, 2, 2:3], 0.0).then_inc(proj_free, PROJ_BANKS)
            pool.memset(small[:, 2, 3:4], 0.0).then_inc(sq_free, SQ_SLOTS)
            pool.memset(small[:, 2, 4:5], 0.0).then_inc(const_ready, 1)
            with pool.Fori(0, DEPTH * LAYER_CHUNKS // RAW_SLOTS) as i:
                for n in range(RAW_SLOTS):
                    pool.wait_ge(w_hi, i * RAW_SLOTS + (n + 1))
                    pool.tensor_tensor(WLO[:, n % 2, :], RAW[:, n, :], WHI[:, n % 2, :], ALU.subtract)\
                        .then_inc(w_split, 1)

        @block.scalar
        def _(act):
            def split_hi(L, c, i=0, per=0):
                n = c % RAW_SLOTS
                assert per % RAW_SLOTS == 0
                act.wait_ge(w_dma[n], (L * (LAYER_CHUNKS // RAW_SLOTS) + i * (per // RAW_SLOTS) + (c // RAW_SLOTS + 1)) * 16)
                act.wait_ge(w_used, L * LAYER_CHUNKS + i * per + (c + 1))
                act.activation(WHI[:, n % 2, :], RAW[:, n, :], ACT.Copy).then_inc(w_hi, 1)

            def square(L, q, src):
                act.wait_ge(sq_free, L * LAYER_SQ + (q + 1))
                act.activation(SQ[:, q % 2, :], src, ACT.Square).then_inc(sq_done, 1)

            def rsqrt_mean(dst, src, count):
                act.activation(dst, src, ACT.Ln, scale=1.0 / count, bias=eps[:, 0:1])
                act.drain()
                return act.activation(dst, dst, ACT.Exp, scale=-0.5)

            def pre(L, s):
                gain = cur[:, P_GAIN + 2 * s * KT:]
                if s == 0:
                    act.wait_ge(cur_ready, L + 1)
                for k in range(KT):
                    act.wait_ge(x_ready, (L * 3 + s) * 8 + (k + 1))
                    act.activation(HHI[:, k, :], X[:, k, :], ACT.Copy, scale=gain[:, k:k + 1]).then_inc(h_hi, 1)
                for k in range(KT):
                    square(L, Q_PRE[s] + k, X[:, k, :])
                act.wait_ge(pre_sum, L * 3 + (s + 1))
                rsqrt_mean(R[:], bank[4][:], D_MODEL).then_inc(pre_r, 1)

            def post(L, s):
                act.wait_ge(post_sum, L * 3 + (s + 1))
                rsqrt_mean(RP[:], bank[4][:], D_MODEL).then_inc(post_r, 1)

            def down(L, s, c0, j0, per, tail_ahead=True):
                def body(i, last):
                    for b in range(4):
                        for n in range(per):
                            if not (last and not tail_ahead and b == 3 and n >= per - 2):
                                split_hi(L, c0 + b * per + n + 2, i, 4 * per)
                        act.wait_ge(proj_free, L * LAYER_JOBS + i * 4 + (j0 + b + 1 + PROJ_BANKS))
                        q = Q_POST[s] + b
                        act.wait_ge(sq_free, L * LAYER_SQ + i * 4 + (q + 1))
                        act.activation(SQ[:, q % 2, :], Y[:, bass.ds(i * 4 + b, 1), :].rearrange("p a n -> p (a n)")
                                       if not isinstance(i, int) else Y[:, i * 4 + b, :], ACT.Square)\
                            .then_inc(sq_done, 1)
                body(0, False)
                body(1, True)
                post(L, s)

            def ffn(L, s):
                c0, j0, c1, j1 = ((C_UP0, J_UP0, C_DOWN0, J_DOWN0), None, (C_UP1, J_UP1, C_DOWN1, J_DOWN1))[s]
                f = s // 2
                act.preload_act_table_set("natural_log_exp_and_others")
                pre(L, s)
                act.preload_act_table_set("silu_and_others")
                with act.Fori(0, FT // 2) as i:
                    for b in range(2):
                        n = (L * 2 + f) * FT + i * 2 + (b + 1)
                        split_hi(L, c0 + 2 * b + 2, i, 4)
                        split_hi(L, c0 + 2 * b + 3, i, 4)
                        act.wait_ge(proj_free, L * LAYER_JOBS + i * 4 + (j0 + 2 * b + 1 + PROJ_BANKS))
                        act.activation(TMP[:], TMP[:], ACT.Silu).then_inc(silu_ready, 1)
                        act.wait_ge(u_ready, n)
                        act.activation(UHI[:, bass.ds(i * 2 + b, 1), :].rearrange("p a n -> p (a n)"), UB[:], ACT.Copy)\
                            .then_inc(u_hi, 1)
                act.preload_act_table_set("natural_log_exp_and_others")
                down(L, s, c1, j1, DOWN_CHUNKS, tail_ahead=(s == 0))

            def mixer(L):
                pre(L, 1)
                for n in range(KV_CHUNKS):
                    split_hi(L, C_KV + n + 2)
                for n in range(4):
                    split_hi(L, C_GROUP0 + n + 2)
                for half in range(2):
                    act.wait_ge(vwin_full, L * 2 + (half + 1))
                    act.activation(vwin[:, 4 * half:4 * half + 4, :].rearrange("p a b -> p (a b)"), bank[6 + half][:],
                                   ACT.Copy).then_inc(vwin_ready, 1)
                with act.Fori(0, NT) as t:
                    it = L * NT + t

                    def ahead(n):
                        split_hi(L, C_GROUPS + n + 2, t, 4)

                    def decays(n):
                        act.wait_ge(exponent, it * STAGES + (n + 1))
                        act.wait_ge(staged, it * STAGES + (n + 1))
                        src, dst = DD[:, n % 2, :], DD[:, 2 + n % 2, :]
                        if n == 0:
                            ins = act.activation(dst, src, ACT.Exp, scale=-1.0)
                        elif n == 1:
                            ins = act.activation(dst, src, ACT.Exp)
                        else:
                            m = HALVES[n - 2]
                            src = src.rearrange("p (b u m) -> p b u m", u=2, m=m)
                            dst = dst.rearrange("p (b u m) -> p b u m", u=2, m=m)
                            act.activation(dst[:, :, 0, :], src[:, :, 0, :], ACT.Exp, scale=-1.0)
                            ins = act.activation(dst[:, :, 1, :], src[:, :, 1, :], ACT.Exp)
                        ins.then_inc(decay, 1)

                    act.preload_act_table_set("sigmoid_and_others")
                    act.wait_ge(proj_free, L * LAYER_JOBS + t * 4 + (J_GROUP0 + 2 + PROJ_BANKS))
                    act.activation(SIGF, PROJ[:, 0, :], ACT.Sigmoid)
                    act.activation(SIGNF, PROJ[:, 0, :], ACT.Sigmoid, scale=-1.0)
                    act.activation(SIGQ, PROJ[:, 1, :], ACT.Sigmoid).then_inc(sig_ready, 1)
                    act.preload_act_table_set("natural_log_exp_and_others")
                    act.wait_ge(logit_ready, it + 1)
                    act.activation(S[:], S[:], ACT.Exp).then_inc(exp_ready, 1)
                    act.wait_ge(fg_ready, it + 1)
                    act.activation(LF, SIGF, ACT.Ln).then_inc(lf_ready, 1)
                    act.wait_ge(bc_ready, it + 1)
                    act.activation(edec[:], BC[:].rearrange("p (c j) -> p c j", c=HCHUNKS)[:, :, P - 1], ACT.Exp)\
                        .then_inc(edec_ready, 1)
                    decays(0)
                    decays(1)
                    ahead(0)
                    for half in range(2):
                        act.wait_ge(pt_full, it * 2 + (half + 1))
                        act.activation(PT[:, 4 * half:4 * half + 4, :].rearrange("p a b -> p (a b)"),
                                       bank[6 + half][:], ACT.Copy).then_inc(pt_ready, 1)
                    decays(2)
                    decays(3)
                    ahead(1)
                    decays(4)
                    decays(5)
                    act.wait_ge(ya_ready, it + 1)
                    act.wait_ge(sq_free, L * LAYER_SQ + t + (Q_YA + 2))
                    act.activation(SQ[:, 0, :], Y[:, bass.ds(t, 1), :].rearrange("p a n -> p (a n)"), ACT.Square)\
                        .then_inc(sq_done, 1)
                    act.wait_ge(vtok_full, it + 1)
                    act.activation(VTOK[:].rearrange("p a b -> p (a b)"), bank[5][:], ACT.Copy).then_inc(vtok_ready, 1)
                    act.wait_ge(kht_full, it + 1)
                    act.activation(KHT[:].rearrange("p a b -> p (a b)"), bank[6][:], ACT.Copy).then_inc(kht_ready, 1)
                    ahead(2)
                    decays(6)
                    decays(7)
                    decays(8)
                    ahead(3)
                act.wait_ge(ya_sum, L + 1)
                rsqrt_mean(RP[:], bank[4][:], ACT_WIDTH).then_inc(ya_r, 1)
                for t in range(NT):
                    act.wait_ge(o_ready, (L + 1) * NT)
                    act.activation(DD[:, t, :], Y[:, NT + t, :], ACT.Square).then_inc(yh_sq, 1)
                for t in range(NT):
                    act.wait_ge(yh_sum, L * NT + (t + 1))
                    rsqrt_mean(DD[:, t, :], bank[YH_BANK[t]][:], HEAD_DIM).then_inc(yh_r, 1)
                act.preload_act_table_set("sigmoid_and_others")
                act.wait_ge(proj_free, L * LAYER_JOBS + (J_OUT + PROJ_BANKS))
                act.activation(GATE[:], G[:], ACT.Sigmoid).then_inc(g_sig, 1)
                for k in range(KT):
                    act.wait_ge(z_ready, L * KT + (k + 1))
                    act.activation(HHI[:, k, :], Y[:, k, :], ACT.Copy).then_inc(z_hi, 1)
                act.preload_act_table_set("natural_log_exp_and_others")
                down(L, 1, C_OUT, J_OUT, 1)

            act.preload_act_table_set("natural_log_exp_and_others")
            act.wait_ge(setup, 1)
            act.activation(lbw[:, 2:4, :], lbw[:, 0:2, :], ACT.Exp).then_inc(setup_act, 1)
            with act.Fori(0, DEPTH) as L:
                split_hi(L, 0)
                split_hi(L, 1)
                ffn(L, 0)
                mixer(L)
                ffn(L, 2)

        @block.tensor
        def _(pe):
            def chunk(L, c, tiles, hi, lo, b, i=0, per=0, h_sem=None, h_value=None):
                slot = c % 2
                assert per % 2 == 0
                pe.wait_ge(w_split, L * LAYER_CHUNKS + i * per + (c + 1 + RAW_SLOTS))
                for at, k, first, last in tiles:
                    if h_sem is not None:
                        pe.wait_ge(h_sem, h_value + (k + 1))
                    w = slice(at * P, at * P + P)
                    pe.matmul(bank[b][:], WHI[:, slot, w], hi[:, k, :], start=first, stop=False)
                    pe.matmul(bank[b][:], WHI[:, slot, w], lo[:, k, :], start=False, stop=False)
                    ins = pe.matmul(bank[b][:], WLO[:, slot, w], hi[:, k, :], start=False, stop=last)
                ins.then_inc(w_used, 1)

            def bank_free(L, j, i=0, per=0, back=PROJ_BANKS):
                pe.wait_ge(proj_free, L * LAYER_JOBS + i * per + (j + 1 + PROJ_BANKS - back))

            FULL = [(k, k, k == 0, k == KT - 1) for k in range(KT)]

            def total(src, b, squares, done, lhs=None):
                pe.wait_ge(*squares)
                pe.matmul(bank[b][:], (lhs or ones)[:], src, start=True, stop=True).then_inc(done, 1)

            def pre_total(L, s):
                total(SS[:], 4, (sq_free, L * LAYER_SQ + (Q_PRE[s] + KT + SQ_SLOTS)), pre_sum)

            def down(L, s, c0, j0, width, hi, lo, h=None):
                per = -(-width // TILES)
                for i in range(2):
                    for b in range(4):
                        bank_free(L, j0 + 4 * i + b)
                        for n in range(per):
                            tiles = [(k - n * TILES, k, k == 0, k == width - 1)
                                     for k in range(n * TILES, min(width, (n + 1) * TILES))]
                            first = h is not None and i == 0 and b == 0
                            chunk(L, c0 + (4 * i + b) * per + n, tiles, hi, lo, b,
                                  h_sem=h[0] if first else None, h_value=h[1] if first else None)
                total(SS[:], 4, (sq_free, L * LAYER_SQ + (Q_POST[s] + KT + SQ_SLOTS)), post_sum)

            def ffn(L, s):
                c0, j0, c1, j1 = ((C_UP0, J_UP0, C_DOWN0, J_DOWN0), None, (C_UP1, J_UP1, C_DOWN1, J_DOWN1))[s]
                h_value = (L * 3 + s) * 8

                def body(i, first):
                    for b in range(2):
                        for g in range(2):
                            n = 2 * b + g
                            bank_free(L, j0 + n, i, 4)
                            chunk(L, c0 + n, FULL, HHI, HLO, n, i, 4,
                                  h_lo if first and n == 0 else None, h_value)
                        if first and b == 0:
                            pre_total(L, s)
                body(0, True)
                with pe.Fori(1, FT // 2) as i:
                    body(i, False)
                pe.wait_ge(u_lo, (L * 2 + (s // 2 + 1)) * FT)
                down(L, s, c1, j1, FT, UHI, ULO)

            def mixer(L):
                for n in range(KV_CHUNKS):
                    if n % 2 == 0:
                        bank_free(L, J_KV + n // 2)
                    ks = [(k - 4 * (n % 2), k, k == 0, k == KT - 1) for k in range(4 * (n % 2), 4 * (n % 2) + 4)]
                    chunk(L, C_KV + n, ks, HHI, HLO, n // 2, h_sem=h_lo if n < 2 else None, h_value=(L * 3 + 1) * 8)
                    if n == 1:
                        pre_total(L, 1)
                for n in range(4):
                    bank_free(L, J_GROUP0 + n, back=2 if n < 2 else 4)
                    chunk(L, C_GROUP0 + n, FULL, HHI, HLO, n)
                pe.wait_ge(proj_free, L * LAYER_JOBS + (J_KV + 2 + PROJ_BANKS))
                for n in range(8):
                    ins = pe.transpose(bank[6 + n // 4][:, (n % 4) * P:(n % 4) * P + P], vT[:, CHUNK * n:CHUNK * n + P], ident[:])
                    if n % 4 == 3:
                        ins.then_inc(vwin_full, 1)
                with pe.Fori(0, NT) as t:
                    it = L * NT + t

                    def next_group(n):
                        bank_free(L, J_GROUPS + n, t, 4)
                        chunk(L, C_GROUPS + n, FULL, HHI, HLO, n, t, 4)

                    pe.wait_ge(proj_free, L * LAYER_JOBS + t * 4 + (J_GROUP0 + 4 + PROJ_BANKS))
                    pe.sem_inc(held)
                    for n in range(8):
                        for h in range(2):
                            rows = slice(64 * h, 64 * h + 64)
                            ins = pe.matmul(bank[4 + n // 4][rows, (n % 4) * P:(n % 4) * P + P],
                                            PROJ[rows, 3, CHUNK * n:CHUNK * n + CHUNK],
                                            kT[rows, CHUNK * n:CHUNK * n + P], start=True, stop=True)
                    ins.then_inc(qk_full, 1)
                    next_group(0)
                    pe.wait_ge(p_ready, it + 1)
                    pe.wait_ge(vwin_ready, L * 2 + 2)
                    for n in range(8):
                        ins = pe.transpose(bank[6 + n // 4][:, (n % 4) * P:(n % 4) * P + P], Slog[:, n, :], ident[:])
                        if n % 4 == 3:
                            ins.then_inc(pt_full, 1)
                    next_group(1)
                    pe.wait_ge(pt_ready, it * 2 + 2)
                    for n in range(8):
                        for h in range(2):
                            rows = slice(64 * h, 64 * h + 64)
                            ins = pe.matmul(bank[4][rows, CHUNK * n:CHUNK * n + CHUNK], vwin[:, n, rows],
                                            PT[:, n, rows], start=True, stop=True)
                    ins.then_inc(pv_full, 1)
                    next_group(2)
                    for c in range(HCHUNKS):
                        ins = pe.transpose(bank[5][:, c * P:c * P + P], PROJ[:, 2, c * P:c * P + P], ident[:])
                    ins.then_inc(vtok_full, 1)
                    pe.wait_ge(staged, it * STAGES + 3)
                    for c in range(HCHUNKS):
                        ins = pe.transpose(bank[6][:, c * P:c * P + P], KH[:, c * P:c * P + P], ident[:])
                    ins.then_inc(kht_full, 1)
                    next_group(3)
                    pe.wait_ge(vtok_ready, it + 1)
                    pe.wait_ge(kht_ready, it + 1)
                    for c in range(HCHUNKS - 1):
                        for h in range(2):
                            rows = slice(64 * h, 64 * h + 64)
                            ins = pe.matmul(bank[7][rows, 64 * c:64 * c + 64], KHT[:, c, rows], VTOK[:, c, rows],
                                            start=True, stop=True)
                    ins.then_inc(ds_full, 1)
                    for n in range(4):
                        b = 4 + 2 * (n % 2)
                        levels = range(2 * n, min(2 * n + 2, NLEV))
                        if n == 0:
                            pe.wait_ge(ya_ready, it + 1)
                        elif n == 1:
                            pe.wait_ge(st_ready, it + 1)
                        else:
                            pe.wait_ge(lv_used, it * 5 + (n - 1))
                        pe.wait_ge(staged, it * STAGES + (levels[-1] + 5))
                        for l in levels:
                            for c in range(HCHUNKS):
                                for h in range(2):
                                    rows = slice(64 * h, 64 * h + 64)
                                    at = (l - 2 * n) * 256 + c * 64
                                    ins = pe.matmul(bank[b + h][:, at:at + 64], KZ[rows, l, c * P:c * P + P],
                                                    QC[rows, l, c, :], start=True, stop=True)
                        ins.then_inc(lv_full, 1)
                    pe.wait_ge(lv_used, it * 5 + 3)
                    for c in range(HCHUNKS):
                        for h in range(2):
                            rows = slice(64 * h, 64 * h + 64)
                            ins = pe.matmul(bank[4 + h][:, c * P:c * P + P], KK[rows, c * P:c * P + P],
                                            PROJ[rows, 1, c * P:c * P + P], start=True, stop=True)
                    ins.then_inc(lv_full, 1)
                    pe.wait_ge(lv_used, it * 5 + 5)
                    for h in range(2):
                        rows = slice(64 * h, 64 * h + 64)
                        for c in range(HCHUNKS):
                            dst = bank[6][rows, c * P:c * P + P]
                            ins = pe.matmul(dst, VTOK[:, c, rows], SM[:, h, c, :], start=True, stop=(c == 0))
                            if c > 0:
                                ins = pe.matmul(dst, ST[rows, c - 1, :], QB[rows, c * P:c * P + P],
                                                start=False, stop=True)
                    ins.then_inc(o_full, 1)
                total(RP[:], 4, (sq_free, L * LAYER_SQ + (Q_YA + NT + SQ_SLOTS)), ya_sum)
                for t in range(NT):
                    if YH_BANK[t] == 4:
                        pe.wait_ge(ya_r, L + 1)
                    total(DD[:, t, :], YH_BANK[t], (yh_sq, L * NT + (t + 1)), yh_sum, block_ones)
                down(L, 1, C_OUT, J_OUT, KT, HHI, HLO, (z_lo, L * 8))

            pe.wait_ge(const_ready, 1)
            pe.wait_ge(setup, 2)
            for n in range(4):
                w = slice(2 * n * RELS, 2 * (n + 1) * RELS)
                ins = pe.matmul(bank[n][0:CHUNK, 0:2 * RELS], ones[0:BUCKETS, 0:CHUNK], oh_rel[:, w], start=True, stop=True)
            ins.then_inc(setup_pe, 1)
            with pe.Fori(0, DEPTH) as L:
                ffn(L, 0)
                mixer(L)
                ffn(L, 2)

        @block.vector
        def _(dve):
            def take(L, c, dst, src, i=0, per=0, jobs_r=True):
                dve.wait_ge(w_used, L * LAYER_CHUNKS + i * per + (c + 1 + SPLIT_SLOTS))
                if jobs_r:
                    return dve.tensor_tensor(dst, src, R[:], ALU.mult)
                return dve.tensor_copy(dst, src)

            def add_square(L, q, acc, slot=None):
                dve.drain()
                dve.wait_ge(sq_done, L * LAYER_SQ + (q + 1))
                dve.tensor_tensor(acc, acc, SQ[:, q % 2 if slot is None else slot, :], ALU.add).then_inc(sq_free, 1)

            def pre(L, s):
                gain = cur[:, P_GAIN + 2 * s * KT:]
                for k in range(KT):
                    dve.wait_ge(h_hi, (L * 3 + s) * 8 + (k + 1))
                    dve.scalar_tensor_tensor(out=HLO[:, k, :], in0=X[:, k, :], scalar=gain[:, k:k + 1],
                                             in1=HHI[:, k, :], op0=ALU.mult, op1=ALU.subtract).then_inc(h_lo, 1)
                dve.memset(SS[:], 0.0)
                for k in range(KT):
                    add_square(L, Q_PRE[s] + k, SS[:])
                dve.wait_ge(pre_r, L * 3 + (s + 1))
                dve.memset(SS[:], 0.0)

            def down(L, s, c0, j0, per):
                for m in range(KT):
                    take(L, c0 + m * per + per - 1, Y[:, m, :], bank[m % 4][:], jobs_r=False).then_inc(proj_free, 1)
                    if m > 0:
                        add_square(L, Q_POST[s] + m - 1, SS[:])
                add_square(L, Q_POST[s] + KT - 1, SS[:])
                gain = cur[:, P_GAIN + (2 * s + 1) * KT:]
                dve.wait_ge(post_r, L * 3 + (s + 1))
                for k in range(KT):
                    dve.scalar_tensor_tensor(out=Y[:, k, :], in0=Y[:, k, :], scalar=gain[:, k:k + 1],
                                             in1=RP[:], op0=ALU.mult, op1=ALU.mult)
                    dve.drain()
                    dve.tensor_tensor(X[:, k, :], X[:, k, :], Y[:, k, :], ALU.add).then_inc(x_ready, 1)

            def ffn(L, s):
                c0, j0, c1, j1 = ((C_UP0, J_UP0, C_DOWN0, J_DOWN0), None, (C_UP1, J_UP1, C_DOWN1, J_DOWN1))[s]
                pre(L, s)
                with dve.Fori(0, FT // 2) as i:
                    for b in range(2):
                        n = (L * 2 + s // 2) * FT + i * 2 + (b + 1)
                        dve.drain()
                        take(L, c0 + 2 * b, TMP[:], bank[2 * b][:], i, 4).then_inc(proj_free, 1)
                        take(L, c0 + 2 * b + 1, UB[:], bank[2 * b + 1][:], i, 4).then_inc(proj_free, 1)
                        dve.drain()
                        dve.wait_ge(silu_ready, n)
                        dve.tensor_tensor(UB[:], UB[:], TMP[:], ALU.mult).then_inc(u_ready, 1)
                        dve.wait_ge(u_hi, n)
                        dve.tensor_tensor(ULO[:, bass.ds(i * 2 + b, 1), :].rearrange("p a n -> p (a n)"), UB[:],
                                          UHI[:, bass.ds(i * 2 + b, 1), :].rearrange("p a n -> p (a n)"), ALU.subtract)\
                            .then_inc(u_lo, 1)
                down(L, s, c1, j1, DOWN_CHUNKS)

            def mixer(L):
                for buf in (KZ, SM):
                    dve.memset(buf[:], 0.0)
                for buf in (kT, vT):
                    dve.memset(buf[:, 0:CHUNK], 0.0)
                pre(L, 1)
                take(L, C_KV + 1, kT[:, CHUNK:], bank[0][:]).then_inc(proj_free, 1)
                take(L, C_KV + 3, vT[:, CHUNK:], bank[1][:]).then_inc(proj_free, 1)
                dve.memset(RP[:], 0.0)
                chunked = lambda a: a.rearrange("p (c j) -> p c j", c=HCHUNKS)
                with dve.Fori(0, NT) as t:
                    it = L * NT + t
                    sink = cur[:, bass.ds(t + P_SINK, 1)]
                    lower, upper = lb[:, bass.ds(t, 1)], lb[:, bass.ds(t + NT, 1)]
                    F, Q, I, QA = (PROJ[:, n, :] for n in range(4))
                    for n in range(4):
                        take(L, C_GROUP0 + n, PROJ[:, n, :], bank[n][:], t, 4).then_inc(proj_free, 1)
                    dve.wait_ge(qk_full, it + 1)
                    bias_t = bias[:, bass.ds(t, 1), :]
                    dve.memset(Slog[:, 0, 0:CHUNK], NEG_INF)
                    for a, z, k0 in ((0, 1, CHUNK), (1, 4, 0), (4, 8, 0)):
                        src = bank[4 + a // 4][:].rearrange("p (n k) -> p n k", n=4)[:, a % 4:a % 4 + z - a, k0:]
                        dve.scalar_tensor_tensor(out=Slog[:, a:z, k0:], in0=src, scalar=HEAD_DIM ** -0.5,
                                                 in1=bias_t[:, :, k0:].to_broadcast([P, z - a, WINDOW - k0]),
                                                 op0=ALU.mult, op1=ALU.add)
                    dve.drain()
                    top = small[:, 0, :]
                    dve.tensor_reduce(top, Slog, AX_X, ALU.max)
                    dve.drain()
                    dve.tensor_scalar(top, top, sink, None, ALU.max)
                    dve.drain()
                    dve.tensor_scalar(Ssink, top, sink, -1.0, ALU.subtract, ALU.mult)
                    dve.tensor_tensor(Slog, Slog, top.unsqueeze(2).to_broadcast([P, 8, WINDOW]), ALU.subtract)\
                        .then_inc(logit_ready, 1)
                    dve.wait_ge(sig_ready, it + 1)
                    dve.tensor_scalar(SIGF, SIGF, upper, lower, ALU.mult, ALU.add)
                    dve.drain()
                    dve.tensor_scalar(SIGF, SIGF, FG_MIN, None, ALU.max).then_inc(fg_ready, 1)
                    dve.tensor_scalar(KK[:], SIGNF, upper, None, ALU.mult)
                    dve.tensor_tensor(Q, Q, SIGQ, ALU.mult)
                    dve.wait_ge(exp_ready, it + 1)
                    total, inverse = small[:, 1, :], small[:, 2, :]
                    dve.tensor_reduce(total, Slog, AX_X, ALU.add)
                    dve.drain()
                    dve.tensor_tensor(total, total, Ssink, ALU.add)
                    dve.drain()
                    dve.reciprocal(inverse, total)
                    dve.drain()
                    dve.tensor_tensor(Slog, Slog, inverse.unsqueeze(2).to_broadcast([P, 8, WINDOW]), ALU.mult)\
                        .then_inc(p_ready, 1)
                    dve.wait_ge(lf_ready, it + 1)
                    for c in range(HCHUNKS):
                        w = slice(c * P, c * P + P)
                        ins = dve.tensor_tensor_scan(BC[:, w], ones[:], LF[:, w], 0.0, ALU.mult, ALU.add)
                    ins.then_inc(bc_ready, 1)
                    dve.drain()

                    def exponents(n):
                        dst = DD[:, n % 2, :]
                        if n == 0:
                            ins = dve.tensor_tensor(chunked(dst), chunked(BC[:]),
                                                    chunked(BC[:])[:, :, P - 1:P].to_broadcast([P, HCHUNKS, P]), ALU.subtract)
                        elif n == 1:
                            ins = dve.tensor_copy(dst, BC[:])
                        else:
                            m = HALVES[n - 2]
                            blocks = BC[:].rearrange("p (b j) -> p b j", j=2 * m)
                            ins = dve.tensor_tensor(dst.rearrange("p (b j) -> p b j", j=2 * m), blocks,
                                                    blocks[:, :, m - 1:m].to_broadcast([P, SEQ // (2 * m), 2 * m]), ALU.subtract)
                        ins.then_inc(exponent, 1)

                    def stage(n):
                        dve.wait_ge(decay, it * STAGES + (n + 1))
                        e = DD[:, 2 + n % 2, :]
                        if n == 0:
                            ins = dve.tensor_tensor(KH[:], KK[:], e, ALU.mult)
                        elif n == 1:
                            ins = dve.tensor_tensor(QB[:], Q, e, ALU.mult)
                        else:
                            l, m = n - 2, HALVES[n - 2]
                            halves = lambda a: a.rearrange("p (b u m) -> p b u m", u=2, m=m)
                            packed = QC[:, l, :, :].rearrange("p c j -> p (c j)").rearrange("p (b m) -> p b m", m=m)
                            dve.tensor_tensor(packed, halves(Q)[:, :, 1, :], halves(e)[:, :, 1, :], ALU.mult)
                            ins = dve.tensor_tensor(halves(KZ[:, l, :])[:, :, 0, :], halves(KK[:])[:, :, 0, :],
                                                    halves(e)[:, :, 0, :], ALU.mult)
                        ins.then_inc(staged, 1)
                        if n + 2 < STAGES:
                            exponents(n + 2)

                    exponents(0)
                    exponents(1)
                    for n in range(6):
                        stage(n)
                    dve.wait_ge(pv_full, it + 1)
                    dve.tensor_copy(Y[:, bass.ds(t, 1), :].rearrange("p a n -> p (a n)"), bank[4][:]).then_inc(ya_ready, 1)
                    for n in range(6, STAGES):
                        stage(n)
                    dve.wait_ge(sq_done, L * LAYER_SQ + t + (Q_YA + 1))
                    dve.tensor_tensor(RP[:], RP[:], SQ[:, 0, :], ALU.add).then_inc(sq_free, 1)
                    dve.wait_ge(ds_full, it + 1)
                    dve.wait_ge(edec_ready, it + 1)
                    dve.tensor_copy(ST[:, 0, :], bank[7][:, 0:64])
                    for c in range(1, HCHUNKS - 1):
                        dve.drain()
                        ins = dve.scalar_tensor_tensor(out=ST[:, c, :], in0=ST[:, c - 1, :], scalar=edec[:, c:c + 1],
                                                       in1=bank[7][:, 64 * c:64 * c + 64], op0=ALU.mult, op1=ALU.add)
                    ins.then_inc(st_ready, 1)
                    for n in range(4):
                        b = 4 + 2 * (n % 2)
                        dve.wait_ge(lv_full, it * 5 + (n + 1))
                        dve.sem_inc(held)
                        for l in range(2 * n, min(2 * n + 2, NLEV)):
                            m = HALVES[l]
                            dve.drain()
                            mask = level_mask[:, 64 * l:64 * l + 64].rearrange("p (b m) -> p b m", m=m)
                            for h in range(2):
                                at = (l - 2 * n) * 256
                                src = bank[b + h][:, at:at + 256].rearrange("p (c b m) -> p c b m", c=HCHUNKS, m=m)
                                dst = SM[:, h, :, :].rearrange("p c (b u m) -> p c b u m", u=2, m=m)[:, :, :, 1, :]
                                ins = dve.copy_predicated(dst, mask.unsqueeze(1).to_broadcast([P, HCHUNKS, 64 // m, m]), src)
                        ins.then_inc(lv_used, 1)
                    dve.drain()
                    dve.wait_ge(lv_full, it * 5 + 5)
                    dve.sem_inc(held)
                    for h in range(2):
                        ins = dve.copy_predicated(SM[:, h, :, :], ident[:].bitcast(U32).unsqueeze(1).to_broadcast([P, HCHUNKS, P]),
                                                  bank[4 + h][:].rearrange("p (c j) -> p c j", c=HCHUNKS))
                    ins.then_inc(lv_used, 1)
                    dve.wait_ge(o_full, it + 1)
                    dve.tensor_copy(Y[:, bass.ds(t + NT, 1), :].rearrange("p a n -> p (a n)"), bank[6][:]).then_inc(o_ready, 1)
                for n in range(NT):
                    take(L, C_GROUPS + 4 * (NT - 1) + n, G[:, n, :], bank[n][:]).then_inc(proj_free, 1)

                def z_low(k):
                    dve.wait_ge(z_hi, L * KT + (k + 1))
                    dve.tensor_tensor(HLO[:, k, :], Y[:, k, :], HHI[:, k, :], ALU.subtract).then_inc(z_lo, 1)
                dve.wait_ge(ya_r, L + 1)
                for k in range(NT):
                    dve.scalar_tensor_tensor(out=Y[:, k, :], in0=Y[:, k, :], scalar=cur[:, P_YA + k:P_YA + k + 1],
                                             in1=RP[:], op0=ALU.mult, op1=ALU.mult).then_inc(z_ready, 1)
                dve.wait_ge(g_sig, L + 1)
                for k in range(NT):
                    dve.tensor_tensor(G[:, k, :], G[:, k, :], GATE[:, k, :], ALU.mult)
                for k in range(NT):
                    z_low(k)
                for k in range(NT):
                    dve.wait_ge(yh_r, L * NT + (k + 1))
                    dve.scalar_tensor_tensor(out=Y[:, NT + k, :], in0=Y[:, NT + k, :], scalar=cur[:, P_YH + k:P_YH + k + 1],
                                             in1=DD[:, k, :], op0=ALU.mult, op1=ALU.mult)
                    dve.drain()
                    dve.tensor_tensor(Y[:, NT + k, :], Y[:, NT + k, :], G[:, k, :], ALU.mult).then_inc(z_ready, 1)
                for k in range(NT):
                    z_low(NT + k)
                down(L, 1, C_OUT, J_OUT, 1)

            dve.wait_ge(const_dma, 16 * 7)
            top = lbw[:, 4, :]
            dve.tensor_tensor(top, par[:, 0, P_LB:P_LB + NT], par[:, 1, P_LB:P_LB + NT], ALU.max)
            dve.drain()
            dve.tensor_tensor(lbw[:, 0, :], par[:, 0, P_LB:P_LB + NT], top, ALU.subtract)
            dve.tensor_tensor(lbw[:, 1, :], par[:, 1, P_LB:P_LB + NT], top, ALU.subtract).then_inc(setup, 1)
            for h in range(HEADS):
                ins = dve.tensor_scalar(oh_rel[:, h * RELS:h * RELS + RELS], oh_sb, rel_sb[:, h:h + 1], None, ALU.mult)
            ins.then_inc(setup, 1)
            dve.wait_ge(setup_act, 1)
            dve.tensor_tensor(lbw[:, 4, :], lbw[:, 2, :], lbw[:, 3, :], ALU.add)
            dve.drain()
            dve.reciprocal(lbw[:, 5, :], lbw[:, 4, :])
            dve.drain()
            dve.tensor_tensor(lbw[:, 0, :], lbw[:, 2, :], lbw[:, 5, :], ALU.mult)
            dve.tensor_tensor(lbw[:, 1, :], lbw[:, 3, :], lbw[:, 5, :], ALU.mult)
            dve.drain()
            dve.tensor_tensor(lb_all[:, 0, 0:NT], lbw[:, 0, :], lbw[:, 0, :], ALU.subtract)
            dve.tensor_tensor(lbw[:, 1, :], lbw[:, 0, :], lbw[:, 1, :], ALU.add)
            dve.drain()
            dve.tensor_tensor(lb_all[:, 1, 0:NT], lbw[:, 1, :], lbw[:, 0, :], ALU.subtract)
            dve.drain()
            dve.tensor_scalar(lb_all[:, :, NT:], lb_all[:, :, 0:NT], -1.0, 1.0, ALU.mult, ALU.add)
            dve.wait_ge(setup_pe, 1)
            for n in range(4):
                ins = dve.tensor_copy(relT[:, 2 * n * RELS:2 * (n + 1) * RELS], bank[n][0:CHUNK, 0:2 * RELS])
            ins.then_inc(setup, 1)
            dve.wait_ge(setup_dma, 48)
            dve.wait_ge(const_ready, 1)
            dve.memset(TMP[:, 0:1], 0.0).then_inc(x_ready, KT)
            dve.memset(TMP[:, 1:2], 0.0).then_inc(staged, 2)
            with dve.Fori(0, DEPTH) as L:
                dve.tensor_copy(cur[:], par[:, bass.ds(L, 1), :].rearrange("p a n -> p (a n)"))
                dve.tensor_copy(lb[:], lb_all[:, bass.ds(L, 1), :].rearrange("p a n -> p (a n)"))
                dve.drain()
                for s in (0, 2):
                    g = cur[:, P_GAIN + (2 * s + 1) * KT:P_GAIN + (2 * s + 2) * KT]
                    ins = dve.tensor_scalar(g, g, 0.5, None, ALU.mult)
                ins.then_inc(cur_ready, 1)
                ffn(L, 0)
                mixer(L)
                ffn(L, 2)


ACT_WIDTH = HEADS * HEAD_DIM
YH_BANK = [5, 6, 7, 4]


def weight_stream(w_ffn_in, w_ffn_out, w_in, w_out):
    def columns(w):
        k, n = w.shape[0] // P, w.shape[1] // P
        return w.reshape(k, P, n, P).transpose(2, 1, 0, 3)

    def chunks(tiles, sizes):
        n = tiles.shape[0]
        out = np.zeros((n, len(sizes), P, TILES, P), tiles.dtype)
        at = 0
        for j, size in enumerate(sizes):
            out[:, j, :, :size, :] = tiles[:, :, at:at + size, :]
            at += size
        return out.reshape(n * len(sizes), P, CW)

    def paired(w, axis):
        order = [t + NT * half for t in range(NT) for half in range(2)]
        shape = w.shape
        w = w.reshape(shape[:axis] + (HEADS, HEAD_DIM) + shape[axis + 1:])
        return np.take(w, order, axis=axis).reshape(shape)

    width, kv = HEADS * HEAD_DIM, 2 * HEAD_DIM
    parts = []
    for layer in range(DEPTH):
        def ffn(j):
            gate_up = columns(w_ffn_in[layer, j])
            order = [n for m in range(FT) for n in (m, FT + m)]
            parts.append(chunks(gate_up[order], [TILES]))
            sizes = [min(TILES, FT - n * TILES) for n in range(DOWN_CHUNKS)]
            parts.append(chunks(columns(w_ffn_out[layer, j]), sizes))

        ffn(0)
        w = w_in[layer]
        at = 0
        cut = []
        for size in (width, kv, kv, width, width, width, width):
            cut.append(w[:, at:at + size])
            at += size
        qa, ka, va, qh, fh, ih, gh = cut
        parts.append(chunks(columns(np.concatenate([ka, va], axis=1)), [4, 4]))
        group = [columns(a) for a in (fh, qh, ih, paired(qa, 1))]
        parts.append(chunks(np.stack(group, axis=1).reshape((-1,) + group[0].shape[1:]), [TILES]))
        parts.append(chunks(columns(gh), [TILES]))
        rows = np.concatenate([paired(w_out[layer, :width], 0), w_out[layer, width:]], axis=0)
        parts.append(chunks(columns(rows), [TILES]))
        ffn(1)
    out = np.concatenate(parts, axis=0)
    assert out.shape == (DEPTH * LAYER_CHUNKS, P, CW)
    return out


def kernel(x, norm_gains, w_ffn_in, w_ffn_out, w_in, w_out, attn_sinks, attn_out_gain,
           rel_bias, hgrn_lb_logits, hgrn_norm_gain):
    import concourse.bacc as bacc
    from concourse.bass_utils import run_bass_kernel_spmd

    def by_partition(a):
        a = np.asarray(a)
        return a.reshape(DEPTH, -1, P).transpose(2, 0, 1)

    ya_gain = np.asarray(attn_out_gain).reshape(DEPTH, 2, NT, HEAD_DIM).transpose(0, 2, 1, 3).reshape(DEPTH, -1)
    params = np.zeros((P, DEPTH, P_COLS), np.float32)
    params[:, :, P_GAIN:P_YA] = by_partition(norm_gains)
    params[:, :, P_YA:P_YH] = by_partition(ya_gain)
    params[:, :, P_YH:P_SINK] = by_partition(hgrn_norm_gain)
    params[:, :, P_LB:P_COLS] = by_partition(hgrn_lb_logits)
    arrays = {
        "xT": np.ascontiguousarray(np.asarray(x)[0].reshape(SEQ, KT, P).transpose(2, 1, 0)),
        "stream": weight_stream(*(np.asarray(w) for w in (w_ffn_in, w_ffn_out, w_in, w_out))),
        "params": params,
        "sinks": np.ascontiguousarray(attn_sinks),
        "rel_bias": np.ascontiguousarray(rel_bias),
        "one_hot": t5_bucket_one_hot(),
        "masks": level_masks(),
    }
    nc = bacc.Bacc("TRN2", target_bir_lowering=False, num_devices=1)
    args = [nc.dram_tensor(n, a.shape, mybir.dt.from_np(a.dtype), kind="ExternalInput").ap() for n, a in arrays.items()]
    out = nc.dram_tensor("yT", (P, KT, SEQ), F32, kind="ExternalOutput").ap()
    build_program(nc, *args, out)
    result = run_bass_kernel_spmd(nc, [arrays], core_ids=[0])
    yT = result.results[0]["yT"]
    return yT.transpose(2, 1, 0).reshape(1, SEQ, D_MODEL)
```

```python
from contextlib import ExitStack

import numpy as np

import concourse.bass as bass
from concourse import mybir
from concourse.alu_op_type import AluOpType as ALU

ACT = mybir.ActivationFunctionType
F32 = mybir.dt.float32
F32R = mybir.dt.float32r
U32 = mybir.dt.uint32
AX_X = mybir.AxisListType.X

P = 128
DEPTH, SEQ, D_MODEL, D_FF = 2, 512, 1024, 2816
HEADS, HEAD_DIM, CHUNK = 8, 64, 64
WINDOW = 2 * CHUNK
KT = D_MODEL // P
FT = D_FF // P
NT = HEADS // 2
BUCKETS, REL_MAX_DIST = 32, 128
NORM_EPS = 1e-6
NEG_INF = -1e30
FG_MIN = 2.0 ** -63

HCHUNKS = SEQ // P
HALVES = [64, 32, 16, 8, 4, 2]
NLEV = len(HALVES)
STAGES = NLEV + 3
DD_SLOTS = 4
F, QA, Q, I = range(4)
SCORE_SETS = NLEV // 2 + 1
RELS = WINDOW + CHUNK - 1

RAW_SLOTS, SPLIT_SLOTS, PROJ_BANKS, SQ_SLOTS = 4, 2, 4, 2
TILES = 8
CW = TILES * P
DOWN_CHUNKS = -(-FT // TILES)
FFN_IN, FFN_OUT = 2 * FT, KT * DOWN_CHUNKS
KV_CHUNKS = 4
C_UP0 = 0
C_DOWN0 = C_UP0 + FFN_IN
C_KV = C_DOWN0 + FFN_OUT
C_GROUP0 = C_KV + KV_CHUNKS
C_GROUPS = C_GROUP0 + 4
C_OUT = C_GROUPS + 4 * NT
C_UP1 = C_OUT + KT
C_DOWN1 = C_UP1 + FFN_IN
LAYER_CHUNKS = C_DOWN1 + FFN_OUT
assert all(c % RAW_SLOTS == 0 for c in (C_DOWN0, C_KV, C_GROUP0, C_OUT, C_UP1, C_DOWN1, LAYER_CHUNKS))

J_UP0 = 0
J_DOWN0 = J_UP0 + FFN_IN
J_KV = J_DOWN0 + KT
J_GROUP0 = J_KV + 2
J_GROUPS = J_GROUP0 + 4
J_OUT = J_GROUPS + 4 * NT
J_UP1 = J_OUT + KT
J_DOWN1 = J_UP1 + FFN_IN
LAYER_JOBS = J_DOWN1 + KT

Q_PRE = [0, 16, 36]
Q_YA = 24
Q_POST = [8, 28, 44]
LAYER_SQ = 52

P_GAIN, P_YA, P_YH, P_SINK, P_LB = 0, 6 * KT, 6 * KT + NT, 6 * KT + 2 * NT, 6 * KT + 3 * NT
P_COLS = P_LB + NT


def t5_bucket_one_hot():
    rel = np.arange(RELS) - (WINDOW - 1)
    nb = BUCKETS // 2
    n, exact = np.abs(rel), nb // 2
    large = exact + (np.log(np.maximum(n, 1) / exact) / np.log(REL_MAX_DIST / exact) * (nb - exact)).astype(np.int32)
    bucket = (rel > 0).astype(np.int32) * nb + np.where(n < exact, n, np.minimum(large, nb - 1))
    return (bucket[None, :] == np.arange(BUCKETS)[:, None]).astype(np.float32)


def level_masks():
    out = np.zeros((P, NLEV, P // 2), np.uint32)
    key = np.arange(P)
    for n, m in enumerate(HALVES):
        for q in range(P // 2):
            out[:, n, q] = (key // (2 * m) == q // m) & (key % (2 * m) < m)
    return out.reshape(P, -1)


def pair_mask():
    key, query = np.arange(P)[:, None], np.arange(P)[None, :]
    return ((key // 2 == query // 2) & (key <= query)).astype(np.uint32)


def build_program(nc, xT, stream, params, sinks, rel_bias, one_hot, masks, out):
    with ExitStack() as ctx:
        def sb(name, shape, dt=F32, scope=ctx):
            return scope.enter_context(nc.sbuf_tensor(name, shape, dt))

        def sem(name):
            return ctx.enter_context(nc.semaphore(name))

        X = sb("X", [P, KT, SEQ])
        HHI = sb("HHI", [P, KT, SEQ], F32R)
        HLO = sb("HLO", [P, KT, SEQ], F32R)
        RAW = sb("RAW", [P, RAW_SLOTS, CW])
        WHI = sb("WHI", [P, SPLIT_SLOTS, CW], F32R)
        WLO = sb("WLO", [P, SPLIT_SLOTS, CW], F32R)
        Y = sb("Y", [P, KT, SEQ])
        R = sb("R", [P, SEQ])
        RP = sb("RP", [P, SEQ])
        SS = sb("SS", [P, SEQ])
        SQ = sb("SQ", [P, SQ_SLOTS, SEQ])
        TMP = sb("TMP", [P, SEQ])
        UB = sb("UB", [P, SEQ])
        ones = sb("ones", [P, P])
        block_ones = sb("block_ones", [P, P])
        ident = sb("ident", [P, P])
        par = sb("par", [P, DEPTH, P_COLS])
        cur = sb("cur", [P, P_COLS])
        bias = sb("bias", [P, NT, WINDOW])
        mask_sb = sb("mask_sb", [P, NLEV * (P // 2) + P], U32)
        pair_sb = mask_sb[:, NLEV * (P // 2):]
        eps = sb("eps", [P, 1])
        lbw = sb("lbw", [P, 6, NT])
        lb_all = sb("lb_all", [P, DEPTH, 2 * NT])
        lb = sb("lb", [P, 2 * NT])
        small = sb("small", [P, 3, 8])
        edec = sb("edec", [P, HCHUNKS])

        with ExitStack() as ffn_scope:
            UHI = sb("UHI", [P, FT, SEQ], F32R, ffn_scope)
            ULO = sb("ULO", [P, FT, SEQ], F32R, ffn_scope)
        kT = sb("kT", [P, CHUNK + SEQ])
        vT = sb("vT", [P, CHUNK + SEQ])
        vwin = sb("vwin", [P, 8, P])
        KZ = sb("KZ", [P, NLEV, SEQ])
        QC = sb("QC", [P, NLEV, HCHUNKS, P // 2])
        SM = sb("SM", [P, 2, HCHUNKS, P])
        S = sb("S", [P, 8 * WINDOW + 8])
        PT = sb("PT", [P, 8, P])
        PROJ = sb("PROJ", [P, 4, SEQ])
        GATE = sb("GATE", [P, 4, SEQ])
        BC = sb("BC", [P, SEQ])
        KK = sb("KK", [P, SEQ])
        DD = sb("DD", [P, 4, SEQ])
        QB = sb("QB", [P, SEQ])
        KH = sb("KH", [P, SEQ])
        KHT = sb("KHT", [P, HCHUNKS, P])
        VTOK = sb("VTOK", [P, HCHUNKS, P])
        ST = sb("ST", [P, HCHUNKS - 1, HEAD_DIM])
        G = sb("G", [P, NT, SEQ])
        Slog = S[:, 0:8 * WINDOW].rearrange("p (n k) -> p n k", n=8)
        Ssink = S[:, 8 * WINDOW:]
        SIGF, SIGNF, SIGQ, LF = (GATE[:, n, :] for n in range(4))

        bank = [ctx.enter_context(nc.psum_tensor(f"bank{n}", [P, SEQ], F32)) for n in range(8)]

        rel_scratch = nc.dram_tensor("rel_scratch", (CHUNK * HEADS * RELS,), F32, kind="Internal").ap()
        relT = KZ[0:CHUNK, 0:3, :].rearrange("p a b -> p (a b)")[:, 0:HEADS * RELS]
        oh_sb = QC[0:BUCKETS, 0, :, :].rearrange("p a b -> p (a b)")[:, 0:RELS]
        rel_sb = small[0:BUCKETS, 0, :]
        oh_rel = Y[0:BUCKETS, 0:3, :].rearrange("p a b -> p (a b)")[:, 0:HEADS * RELS]

        w_dma = [sem(f"w_dma{n}") for n in range(RAW_SLOTS)]
        w_hi = sem("w_hi")
        w_split = sem("w_split")
        w_used = sem("w_used")
        proj_free = sem("proj_free")
        sq_done = sem("sq_done")
        sq_free = sem("sq_free")
        const_dma = sem("const_dma")
        const_ready = sem("const_ready")
        setup = sem("setup")
        setup_act = sem("setup_act")
        setup_pe = sem("setup_pe")
        setup_dma = sem("setup_dma")
        cur_ready = sem("cur_ready")
        x_ready = sem("x_ready")
        h_hi = sem("h_hi")
        h_lo = sem("h_lo")
        pre_sum = sem("pre_sum")
        pre_r = sem("pre_r")
        post_r = sem("post_r")
        silu_ready = sem("silu_ready")
        u_ready = sem("u_ready")
        u_hi = sem("u_hi")
        u_lo = sem("u_lo")
        pad_ready = sem("pad_ready")
        vwin_full = sem("vwin_full")
        vwin_ready = sem("vwin_ready")
        qk_full = sem("qk_full")
        logit_ready = sem("logit_ready")
        exp_ready = sem("exp_ready")
        p_ready = sem("p_ready")
        pt_full = sem("pt_full")
        pt_ready = sem("pt_ready")
        pv_full = sem("pv_full")
        ya_ready = sem("ya_ready")
        sig_ready = sem("sig_ready")
        fg_ready = sem("fg_ready")
        lf_ready = sem("lf_ready")
        bc_ready = sem("bc_ready")
        edec_ready = sem("edec_ready")
        exponent = sem("exponent")
        decay = sem("decay")
        staged = sem("staged")
        vtok_full = sem("vtok_full")
        vtok_ready = sem("vtok_ready")
        kht_full = sem("kht_full")
        kht_ready = sem("kht_ready")
        ds_full = sem("ds_full")
        st_ready = sem("st_ready")
        lv_full = sem("lv_full")
        lv_used = sem("lv_used")
        o_full = sem("o_full")
        o_ready = sem("o_ready")
        g_sig = sem("g_sig")
        ya_sum = sem("ya_sum")
        ya_r = sem("ya_r")
        yh_sq = sem("yh_sq")
        yh_sum = sem("yh_sum")
        yh_r = sem("yh_r")
        z_ready = sem("z_ready")
        z_hi = sem("z_hi")
        z_lo = sem("z_lo")
        stored = sem("stored")
        held = sem("held")

        block = ctx.enter_context(nc.Block())

        @block.sync
        def _(sp):
            sp.dma_start(par[:], params).then_inc(const_dma, 16)
            for half in range(2):
                dst = par[half * 64:half * 64 + 64, :, P_SINK:P_SINK + NT]
                src = sinks[:, half * NT:half * NT + NT].unsqueeze(0).to_broadcast([64, DEPTH, NT])
                sp.wait_ge(const_dma, 16 * (1 + half))
                sp.dma_start(dst, src).then_inc(const_dma, 16)
            sp.dma_start(rel_sb, rel_bias).then_inc(const_dma, 16)
            sp.dma_start(oh_sb, one_hot).then_inc(const_dma, 16)
            sp.dma_start(mask_sb[:], masks).then_inc(const_dma, 16)
            sp.dma_start(X[:], xT).then_inc(const_dma, 16)
            for n in range(RAW_SLOTS):
                sp.dma_start(RAW[:, n, :], stream[n]).then_inc(w_dma[n], 16)
            sp.wait_ge(setup, 3)
            sp.dma_start(rel_scratch.rearrange("(q c) -> q c", q=CHUNK), relT).then_inc(setup_dma, 16)
            sp.wait_ge(setup_dma, 16)
            for half in range(2):
                base = half * NT * RELS + CHUNK - 1
                src = bass.AP(tensor=rel_scratch.tensor, offset=base,
                              ap=[[HEADS * RELS - 1, CHUNK], [RELS, NT], [1, WINDOW]])
                sp.dma_start(bias[half * 64:half * 64 + 64, :, :], src).then_inc(setup_dma, 16)
            with sp.Fori(1, DEPTH * LAYER_CHUNKS // RAW_SLOTS) as i:
                for n in range(RAW_SLOTS):
                    sp.wait_ge(w_split, i * RAW_SLOTS + (n + 1))
                    sp.dma_start(RAW[:, n, :], stream[i * RAW_SLOTS + n]).then_inc(w_dma[n], 16)
            for k in range(KT):
                sp.wait_ge(x_ready, 8 * (3 * DEPTH) + k + 1)
                sp.dma_start(out[:, k, :], X[:, k, :]).then_inc(stored, 16)
            sp.wait_ge(stored, 16 * KT)

        @block.gpsimd
        def _(pool):
            pool.memset(eps[:], NORM_EPS)
            pool.memset(ones[:], 1.0)
            pool.memset(block_ones[:], 0.0)
            pool.memset(ident[:], 0.0)
            pool.drain()
            for h in range(2):
                pool.memset(block_ones[64 * h:64 * h + 64, 64 * h:64 * h + 64], 1.0)
                pool.drain()
            pool.affine_select(out=ident[:], in_=ident[:], compare_op=ALU.not_equal, fill=1.0, base=0,
                               pattern=[[-1, P]], channel_multiplier=1)
            pool.drain()
            pool.memset(small[:, 2, 0:1], 0.0).then_inc(w_split, RAW_SLOTS)
            pool.memset(small[:, 2, 1:2], 0.0).then_inc(w_used, SPLIT_SLOTS)
            pool.memset(small[:, 2, 2:3], 0.0).then_inc(proj_free, PROJ_BANKS)
            pool.memset(small[:, 2, 3:4], 0.0).then_inc(sq_free, SQ_SLOTS)
            pool.memset(small[:, 2, 5:6], 0.0).then_inc(o_ready, 1)
            pool.memset(small[:, 2, 4:5], 0.0).then_inc(const_ready, 1)

            def split_lo(L, c, i=0, per=0):
                n = c % RAW_SLOTS
                pool.wait_ge(w_hi, L * LAYER_CHUNKS + i * per + (c + 1))
                pool.tensor_tensor(WLO[:, n % 2, :], RAW[:, n, :], WHI[:, n % 2, :], ALU.subtract).then_inc(w_split, 1)

            def exponents(n, it):
                if n >= DD_SLOTS:
                    pool.wait_ge(staged, it * STAGES + (n - DD_SLOTS + 1))
                dst = DD[:, n % DD_SLOTS, :]
                if n == 1:
                    chunked = lambda a: a.rearrange("p (c j) -> p c j", c=HCHUNKS)
                    ins = pool.tensor_tensor(chunked(dst), chunked(BC[:]),
                                             chunked(BC[:])[:, :, P - 1:P].to_broadcast([P, HCHUNKS, P]), ALU.subtract)
                else:
                    m = HALVES[n - 2] if n < STAGES - 1 else 1
                    blocks = BC[:].rearrange("p (b j) -> p b j", j=2 * m)
                    ins = pool.tensor_tensor(dst.rearrange("p (b j) -> p b j", j=2 * m), blocks,
                                             blocks[:, :, m - 1:m].to_broadcast([P, SEQ // (2 * m), 2 * m]), ALU.subtract)
                ins.then_inc(exponent, 1)

            with pool.Fori(0, DEPTH) as L:
                with pool.Fori(0, (C_GROUPS + 2) // RAW_SLOTS) as i:
                    for n in range(RAW_SLOTS):
                        split_lo(L, n, i, RAW_SLOTS)
                for c in range((C_GROUPS + 2) // RAW_SLOTS * RAW_SLOTS, C_GROUPS + 2):
                    split_lo(L, c)
                with pool.Fori(0, NT) as t:
                    it = L * NT + t
                    split_lo(L, C_GROUPS + 2, t, 4)
                    pool.wait_ge(bc_ready, it + 1)
                    for n in range(1, 6):
                        exponents(n, it)
                    split_lo(L, C_GROUPS + 3, t, 4)
                    for n in range(6, STAGES):
                        exponents(n, it)
                    split_lo(L, C_GROUPS + 4, t, 4)
                    split_lo(L, C_GROUPS + 5, t, 4)
                for c in range(C_OUT + 2, C_OUT + 4):
                    split_lo(L, c)
                with pool.Fori(0, (LAYER_CHUNKS - C_OUT - 4) // RAW_SLOTS) as i:
                    for n in range(RAW_SLOTS):
                        split_lo(L, C_OUT + 4 + n, i, RAW_SLOTS)

        @block.scalar
        def _(act):
            def split_hi(L, c, i=0, per=0):
                n = c % RAW_SLOTS
                assert per % RAW_SLOTS == 0
                act.wait_ge(w_dma[n], (L * (LAYER_CHUNKS // RAW_SLOTS) + i * (per // RAW_SLOTS) + (c // RAW_SLOTS + 1)) * 16)
                act.wait_ge(w_used, L * LAYER_CHUNKS + i * per + (c + 1))
                act.activation(WHI[:, n % 2, :], RAW[:, n, :], ACT.Copy).then_inc(w_hi, 1)

            def square(L, q, src):
                act.wait_ge(sq_free, L * LAYER_SQ + (q + 1))
                act.activation(SQ[:, q % 2, :], src, ACT.Square).then_inc(sq_done, 1)

            def rsqrt_mean(dst, src, count):
                act.activation(dst, src, ACT.Ln, scale=1.0 / count, bias=eps[:, 0:1])
                act.drain()
                return act.activation(dst, dst, ACT.Exp, scale=-0.5)

            def pre(L, s, c0):
                gain = cur[:, P_GAIN + 2 * s * KT:]
                if s == 0:
                    act.wait_ge(cur_ready, L + 1)
                for k in range(KT):
                    act.wait_ge(x_ready, (L * 3 + s) * 8 + (k + 1))
                    act.activation(HHI[:, k, :], X[:, k, :], ACT.Copy, scale=gain[:, k:k + 1]).then_inc(h_hi, 1)
                    if k > 0:
                        square(L, Q_PRE[s] + k - 1, X[:, k - 1, :])
                    if k in (3, 5):
                        split_hi(L, c0 + (k + 1) // 2)
                square(L, Q_PRE[s] + KT - 1, X[:, KT - 1, :])
                split_hi(L, c0 + 4)
                act.wait_ge(pre_sum, L * 3 + (s + 1))
                rsqrt_mean(R[:], bank[4][:], D_MODEL).then_inc(pre_r, 1)

            def down(L, s, c0, j0, per, tail_ahead=True, k_outer=False):
                def body(i, last):
                    for b in range(4):
                        for n in range(per):
                            if k_outer and i == 0:
                                if b == 0:
                                    split_hi(L, c0 + 5)
                            elif not (last and not tail_ahead and b == 3 and n >= per - 2):
                                split_hi(L, c0 + b * per + n + 2, i, 4 * per)
                        q = Q_POST[s] + b
                        if last and b == 3:
                            act.wait_ge(w_used, L * LAYER_CHUNKS + (c0 + KT * per + SPLIT_SLOTS))
                            src = bank[3][:]
                        else:
                            act.wait_ge(proj_free, L * LAYER_JOBS + i * 4 + (j0 + b + 1 + PROJ_BANKS))
                            src = Y[:, i * 4 + b, :]
                        act.wait_ge(sq_free, L * LAYER_SQ + i * 4 + (q + 1))
                        act.activation(SQ[:, q % 2, :], src, ACT.Square).then_inc(sq_done, 1)
                body(0, False)
                body(1, True)
                act.wait_ge(sq_free, L * LAYER_SQ + (Q_POST[s] + KT + SQ_SLOTS))
                rsqrt_mean(RP[:], bank[4][:], D_MODEL).then_inc(post_r, 1)

            def ffn(L, s):
                c0, j0, c1, j1 = ((C_UP0, J_UP0, C_DOWN0, J_DOWN0), None, (C_UP1, J_UP1, C_DOWN1, J_DOWN1))[s]
                f = s // 2
                act.preload_act_table_set("natural_log_exp_and_others")
                pre(L, s, c0)
                act.preload_act_table_set("silu_and_others")

                def body(i, first):
                    for b in range(2):
                        n = (L * 2 + f) * FT + i * 2 + (b + 1)
                        if not first:
                            split_hi(L, c0 + 2 * b + 2, i, 4)
                            split_hi(L, c0 + 2 * b + 3, i, 4)
                        elif b == 0:
                            split_hi(L, c0 + 5)
                        act.wait_ge(proj_free, L * LAYER_JOBS + i * 4 + (j0 + 2 * b + 1 + PROJ_BANKS))
                        act.activation(TMP[:], TMP[:], ACT.Silu).then_inc(silu_ready, 1)
                        act.wait_ge(u_ready, n)
                        u = UHI[:, b, :] if first else UHI[:, bass.ds(i * 2 + b, 1), :].rearrange("p a n -> p (a n)")
                        act.activation(u, UB[:], ACT.Copy).then_inc(u_hi, 1)
                body(0, True)
                with act.Fori(1, FT // 2) as i:
                    body(i, False)
                act.preload_act_table_set("natural_log_exp_and_others")
                down(L, s, c1, j1, DOWN_CHUNKS, tail_ahead=(s == 0))

            def mixer(L):
                pre(L, 1, C_KV)
                split_hi(L, C_KV + 5)
                for n in range(4):
                    split_hi(L, C_GROUP0 + n + 2)
                for half in range(2):
                    act.wait_ge(vwin_full, L * 2 + (half + 1))
                    act.activation(vwin[:, 4 * half:4 * half + 4, :].rearrange("p a b -> p (a b)"), bank[6 + half][:],
                                   ACT.Copy).then_inc(vwin_ready, 1)
                with act.Fori(0, NT) as t:
                    it = L * NT + t

                    def ahead(n):
                        split_hi(L, C_GROUPS + n + 2, t, 4)

                    def decays(n):
                        dst = DD[:, n % DD_SLOTS, :]
                        if n > 0:
                            act.wait_ge(exponent, it * (STAGES - 1) + n)
                        if n == 0:
                            ins = act.activation(dst, BC[:], ACT.Exp)
                        elif n == 1:
                            ins = act.activation(dst, dst, ACT.Exp, scale=-1.0)
                        elif n == STAGES - 1:
                            act.wait_ge(staged, it * STAGES + (STAGES - 2))
                            act.activation(DD[:, 1, :], dst, ACT.Exp, scale=-1.0)
                            ins = act.activation(DD[:, 2, :], dst, ACT.Exp)
                        else:
                            m = HALVES[n - 2]
                            dst = dst.rearrange("p (b u m) -> p b u m", u=2, m=m)
                            act.activation(dst[:, :, 0, :], dst[:, :, 0, :], ACT.Exp, scale=-1.0)
                            ins = act.activation(dst[:, :, 1, :], dst[:, :, 1, :], ACT.Exp)
                        ins.then_inc(decay, 1)

                    act.preload_act_table_set("sigmoid_and_others")
                    act.wait_ge(proj_free, L * LAYER_JOBS + t * 4 + (J_GROUP0 + 3 + PROJ_BANKS))
                    act.activation(SIGF, PROJ[:, F, :], ACT.Sigmoid)
                    act.activation(SIGNF, PROJ[:, F, :], ACT.Sigmoid, scale=-1.0)
                    act.activation(SIGQ, PROJ[:, Q, :], ACT.Sigmoid).then_inc(sig_ready, 1)
                    act.preload_act_table_set("natural_log_exp_and_others")
                    act.wait_ge(fg_ready, it + 1)
                    act.activation(LF, SIGF, ACT.Ln).then_inc(lf_ready, 1)
                    ahead(0)
                    act.wait_ge(logit_ready, it + 1)
                    act.activation(S[:], S[:], ACT.Exp).then_inc(exp_ready, 1)
                    act.wait_ge(bc_ready, it + 1)
                    act.activation(edec[:], BC[:].rearrange("p (c j) -> p c j", c=HCHUNKS)[:, :, P - 1], ACT.Exp)\
                        .then_inc(edec_ready, 1)
                    for n in range(3):
                        decays(n)
                    for half in range(2):
                        act.wait_ge(pt_full, it * 2 + (half + 1))
                        act.activation(PT[:, 4 * half:4 * half + 4, :].rearrange("p a b -> p (a b)"),
                                       bank[6 + half][:], ACT.Copy).then_inc(pt_ready, 1)
                    act.wait_ge(vtok_full, it + 1)
                    act.activation(VTOK[:].rearrange("p a b -> p (a b)"), bank[5][:], ACT.Copy).then_inc(vtok_ready, 1)
                    ahead(1)
                    decays(3)
                    act.wait_ge(pv_full, it + 1)
                    act.wait_ge(sq_free, L * LAYER_SQ + t + (Q_YA + 2))
                    act.activation(SQ[:, 0, :], bank[4][:], ACT.Square).then_inc(sq_done, 1)
                    act.activation(Y[:, bass.ds(t, 1), :].rearrange("p a n -> p (a n)"), bank[4][:], ACT.Copy)\
                        .then_inc(ya_ready, 1)
                    act.wait_ge(kht_full, it + 1)
                    act.activation(KHT[:].rearrange("p a b -> p (a b)"), bank[6][:], ACT.Copy).then_inc(kht_ready, 1)
                    for n in range(4, STAGES):
                        decays(n)
                    ahead(2)
                    act.wait_ge(o_full, it + 1)
                    act.activation(Y[:, bass.ds(t + NT, 1), :].rearrange("p a n -> p (a n)"), bank[6][:], ACT.Copy)\
                        .then_inc(o_ready, 1)
                    ahead(3)
                def z_high(k):
                    act.wait_ge(z_ready, L * KT + (k + 1))
                    act.activation(HHI[:, k, :], Y[:, k, :], ACT.Copy).then_inc(z_hi, 1)

                act.wait_ge(ya_sum, L + 1)
                rsqrt_mean(RP[:], bank[4][:], ACT_WIDTH).then_inc(ya_r, 1)
                for t in range(NT):
                    z_high(t)
                    act.wait_ge(o_ready, L * NT + (NT + 1))
                    act.activation(DD[:, t, :], Y[:, NT + t, :], ACT.Square).then_inc(yh_sq, 1)
                for t in range(NT):
                    act.wait_ge(yh_sum, L * NT + (t + 1))
                    rsqrt_mean(DD[:, t, :], bank[YH_BANK[t]][:], HEAD_DIM).then_inc(yh_r, 1)
                act.preload_act_table_set("sigmoid_and_others")
                for t in range(NT):
                    act.wait_ge(proj_free, L * LAYER_JOBS + (J_OUT + PROJ_BANKS))
                    act.activation(GATE[:, t, :], G[:, t, :], ACT.Sigmoid).then_inc(g_sig, 1)
                split_hi(L, C_OUT + 2)
                for k in range(NT, KT):
                    z_high(k)
                    if k == 5:
                        split_hi(L, C_OUT + 3)
                split_hi(L, C_OUT + 4)
                act.preload_act_table_set("natural_log_exp_and_others")
                down(L, 1, C_OUT, J_OUT, 1, k_outer=True)

            act.preload_act_table_set("natural_log_exp_and_others")
            act.wait_ge(setup, 1)
            act.activation(lbw[:, 2:4, :], lbw[:, 0:2, :], ACT.Exp).then_inc(setup_act, 1)
            with act.Fori(0, DEPTH) as L:
                split_hi(L, 0)
                split_hi(L, 1)
                ffn(L, 0)
                mixer(L)
                ffn(L, 2)

        @block.tensor
        def _(pe):
            def chunk(L, c, tiles, hi, lo, b, i=0, per=0, h_sem=None, h_value=None,
                      ready=True, done=True):
                slot = c % 2
                assert per % 2 == 0
                if ready:
                    pe.wait_ge(w_split, L * LAYER_CHUNKS + i * per + (c + 1 + RAW_SLOTS))
                for at, k, first, last in tiles:
                    if h_sem is not None:
                        pe.wait_ge(h_sem, h_value + (k + 1))
                    w = slice(at * P, at * P + P)
                    pe.matmul(bank[b][:], WHI[:, slot, w], hi[:, k, :], start=first, stop=False)
                    pe.matmul(bank[b][:], WHI[:, slot, w], lo[:, k, :], start=False, stop=False)
                    ins = pe.matmul(bank[b][:], WLO[:, slot, w], hi[:, k, :], start=False, stop=last)
                if done:
                    ins.then_inc(w_used, 1)

            def bank_free(L, j, i=0, per=0, back=PROJ_BANKS):
                pe.wait_ge(proj_free, L * LAYER_JOBS + i * per + (j + 1 + PROJ_BANKS - back))

            FULL = [(k, k, k == 0, k == KT - 1) for k in range(KT)]

            def four(L, c0, banks, h_sem, h_value, between=None):
                for k in range(KT):
                    for j in range(4):
                        chunk(L, c0 + k // 2, [(k % 2 * 4 + j, k, k == 0, k == KT - 1)], HHI, HLO, banks[j],
                              h_sem=h_sem if j == 0 else None, h_value=h_value,
                              ready=k % 2 == 0 and j == 0, done=k % 2 == 1 and j == 3)
                        if between is not None:
                            between(k, j)

            def total(src, b, squares, done, lhs=None):
                pe.wait_ge(*squares)
                pe.matmul(bank[b][:], (lhs or ones)[:], src, start=True, stop=True).then_inc(done, 1)

            def pre_total(L, s):
                def at(k, j):
                    if (k, j) == (KT - 1, 1):
                        total(SS[:], 4, (sq_free, L * LAYER_SQ + (Q_PRE[s] + KT + SQ_SLOTS)), pre_sum)
                return at

            def down(L, s, c0, j0, width, hi, lo, h=None, k_outer=None):
                per = -(-width // TILES)
                for m in range(KT):
                    b = m % 4
                    if k_outer is not None and m < 4:
                        if m == 0:
                            bank_free(L, j0 + 3)
                            four(L, c0, range(4), *h, between=k_outer)
                        continue
                    bank_free(L, j0 + m)
                    for n in range(per):
                        tiles = [(k - n * TILES, k, k == 0, k == width - 1)
                                 for k in range(n * TILES, min(width, (n + 1) * TILES))]
                        c = c0 + m * per + n
                        if m < KT - 1 or n < per - 1:
                            first = h is not None and m == 0
                            chunk(L, c, tiles, hi, lo, b, h_sem=h[0] if first else None, h_value=h[1] if first else None)
                        else:
                            chunk(L, c, tiles[:-1], hi, lo, b, done=False)
                            pe.wait_ge(sq_free, L * LAYER_SQ + (Q_POST[s] + KT - 1 + SQ_SLOTS))
                            pe.matmul(bank[4][:], ones[:], SS[:], start=True, stop=False)
                            chunk(L, c, tiles[-1:], hi, lo, b, ready=False)
                pe.wait_ge(sq_done, L * LAYER_SQ + (Q_POST[s] + KT))
                pe.matmul(bank[4][:], ones[:], SQ[:, (Q_POST[s] + KT - 1) % 2, :], start=False, stop=True).then_inc(sq_free, 1)

            def ffn(L, s):
                c0, j0, c1, j1 = ((C_UP0, J_UP0, C_DOWN0, J_DOWN0), None, (C_UP1, J_UP1, C_DOWN1, J_DOWN1))[s]
                bank_free(L, j0 + 3)
                four(L, c0, range(4), h_lo, (L * 3 + s) * 8, pre_total(L, s))
                with pe.Fori(1, FT // 2) as i:
                    for n in range(4):
                        bank_free(L, j0 + n, i, 4)
                        chunk(L, c0 + n, FULL, HHI, HLO, n, i, 4)
                down(L, s, c1, j1, FT, UHI, ULO, (u_lo, (L * 2 + s // 2) * FT))

            def mixer(L):
                bank_free(L, J_KV, back=1)
                four(L, C_KV, range(4), h_lo, (L * 3 + 1) * 8, pre_total(L, 1))
                for n in range(4):
                    if n % 2 == 0:
                        bank_free(L, J_KV + 1 + n // 2, back=1)
                    ks = FULL[4 * (n % 2):4 * (n % 2) + 4]
                    chunk(L, C_GROUP0 + n, [(k - ks[0][1], k, first, last) for _, k, first, last in ks],
                          HHI, HLO, 2 + n // 2)
                pe.wait_ge(pad_ready, L + 1)
                for n in range(8):
                    ins = pe.transpose(bank[6 + n // 4][:, (n % 4) * P:(n % 4) * P + P], vT[:, CHUNK * n:CHUNK * n + P], ident[:])
                    if n % 4 == 3:
                        ins.then_inc(vwin_full, 1)
                with pe.Fori(0, NT) as t:
                    it = L * NT + t

                    def next_group(n, k0=0, k1=KT):
                        if k0 == 0:
                            bank_free(L, J_GROUPS + n, t, 4)
                        chunk(L, C_GROUPS + n, FULL[k0:k1], HHI, HLO, n, t, 4, ready=k0 == 0, done=k1 == KT)

                    def scores(l):
                        n = l // 2
                        b = 4 + 2 * (n % 2)
                        if l == 0:
                            pe.wait_ge(ya_ready, it + 1)
                        elif l == 2:
                            pe.wait_ge(st_ready, it + 1)
                        elif l % 2 == 0:
                            pe.wait_ge(lv_used, it * SCORE_SETS + (n - 1))
                        pe.wait_ge(staged, it * STAGES + (l + 3))
                        for c in range(HCHUNKS):
                            for h in range(2):
                                rows = slice(64 * h, 64 * h + 64)
                                if l < NLEV:
                                    at = (l % 2) * 256 + c * 64
                                    ins = pe.matmul(bank[b + h][:, at:at + 64], KZ[rows, l, c * P:c * P + P],
                                                    QC[rows, l, c, :], start=True, stop=True)
                                else:
                                    ins = pe.matmul(bank[b + h][:, c * P:c * P + P], KK[rows, c * P:c * P + P],
                                                    PROJ[rows, Q, c * P:c * P + P], start=True, stop=True)
                        if l % 2 == 1 or l == NLEV:
                            ins.then_inc(lv_full, 1)

                    next_group(0, 0, 4)
                    pe.wait_ge(proj_free, L * LAYER_JOBS + t * 4 + (J_GROUP0 + 2 + PROJ_BANKS))
                    pe.sem_inc(held)
                    for n in range(8):
                        for h in range(2):
                            rows = slice(64 * h, 64 * h + 64)
                            ins = pe.matmul(bank[4 + n // 4][rows, (n % 4) * P:(n % 4) * P + P],
                                            PROJ[rows, QA, CHUNK * n:CHUNK * n + CHUNK],
                                            kT[rows, CHUNK * n:CHUNK * n + P], start=True, stop=True)
                    ins.then_inc(qk_full, 1)
                    next_group(0, 4, 8)
                    next_group(1)
                    next_group(2, 0, 3)
                    pe.wait_ge(p_ready, it + 1)
                    pe.wait_ge(o_ready, it + 1)
                    pe.wait_ge(vwin_ready, L * 2 + 2)
                    for n in range(8):
                        ins = pe.transpose(bank[6 + n // 4][:, (n % 4) * P:(n % 4) * P + P], Slog[:, n, :], ident[:])
                        if n % 4 == 3:
                            ins.then_inc(pt_full, 1)
                    for c in range(HCHUNKS):
                        ins = pe.transpose(bank[5][:, c * P:c * P + P], PROJ[:, I, c * P:c * P + P], ident[:])
                    ins.then_inc(vtok_full, 1)
                    next_group(2, 3, 4)
                    pe.wait_ge(pt_ready, it * 2 + 2)
                    for n in range(8):
                        for h in range(2):
                            rows = slice(64 * h, 64 * h + 64)
                            ins = pe.matmul(bank[4][rows, CHUNK * n:CHUNK * n + CHUNK], vwin[:, n, rows],
                                            PT[:, n, rows], start=True, stop=True)
                    ins.then_inc(pv_full, 1)
                    pe.wait_ge(staged, it * STAGES + 2)
                    for c in range(HCHUNKS):
                        ins = pe.transpose(bank[6][:, c * P:c * P + P], KH[:, c * P:c * P + P], ident[:])
                    ins.then_inc(kht_full, 1)
                    next_group(2, 4, 6)
                    pe.wait_ge(vtok_ready, it + 1)
                    pe.wait_ge(kht_ready, it + 1)
                    for c in range(HCHUNKS - 1):
                        for h in range(2):
                            rows = slice(64 * h, 64 * h + 64)
                            ins = pe.matmul(bank[7][rows, 64 * c:64 * c + 64], KHT[:, c, rows], VTOK[:, c, rows],
                                            start=True, stop=True)
                    ins.then_inc(ds_full, 1)
                    scores(0)
                    next_group(2, 6, 7)
                    scores(1)
                    next_group(2, 7, 8)
                    scores(2)
                    next_group(3, 0, 1)
                    scores(3)
                    next_group(3, 1, 2)
                    scores(4)
                    next_group(3, 2, 4)
                    scores(5)
                    next_group(3, 4, 5)
                    scores(6)
                    next_group(3, 5, 7)
                    pe.wait_ge(lv_used, (it + 1) * SCORE_SETS)
                    for h in range(2):
                        rows = slice(64 * h, 64 * h + 64)
                        for c in range(HCHUNKS):
                            dst = bank[6][rows, c * P:c * P + P]
                            ins = pe.matmul(dst, VTOK[:, c, rows], SM[:, h, c, :], start=True, stop=(c == 0))
                            if c > 0:
                                ins = pe.matmul(dst, ST[rows, c - 1, :], QB[rows, c * P:c * P + P],
                                                start=False, stop=True)
                    ins.then_inc(o_full, 1)
                    next_group(3, 7, 8)
                total(RP[:], 4, (sq_free, L * LAYER_SQ + (Q_YA + NT + SQ_SLOTS)), ya_sum)

                def yh_total(k, j):
                    if k < NT and j == 3:
                        total(DD[:, k, :], YH_BANK[k], (yh_sq, L * NT + (k + 1)), yh_sum, block_ones)
                down(L, 1, C_OUT, J_OUT, KT, HHI, HLO, (z_lo, L * 8), k_outer=yh_total)

            pe.wait_ge(const_ready, 1)
            pe.wait_ge(setup, 2)
            for n in range(4):
                w = slice(2 * n * RELS, 2 * (n + 1) * RELS)
                ins = pe.matmul(bank[n][0:CHUNK, 0:2 * RELS], ones[0:BUCKETS, 0:CHUNK], oh_rel[:, w], start=True, stop=True)
            ins.then_inc(setup_pe, 1)
            with pe.Fori(0, DEPTH) as L:
                ffn(L, 0)
                mixer(L)
                ffn(L, 2)

        @block.vector
        def _(dve):
            def take(L, c, dst, src, i=0, per=0, jobs_r=True):
                dve.wait_ge(w_used, L * LAYER_CHUNKS + i * per + (c + 1 + SPLIT_SLOTS))
                if jobs_r:
                    return dve.tensor_tensor(dst, src, R[:], ALU.mult)
                return dve.tensor_copy(dst, src)

            def add_square(L, q, acc, slot=None):
                dve.drain()
                dve.wait_ge(sq_done, L * LAYER_SQ + (q + 1))
                dve.tensor_tensor(acc, acc, SQ[:, q % 2 if slot is None else slot, :], ALU.add).then_inc(sq_free, 1)

            def low(L, s, k):
                gain = cur[:, P_GAIN + 2 * s * KT:]
                dve.wait_ge(h_hi, (L * 3 + s) * 8 + (k + 1))
                dve.scalar_tensor_tensor(out=HLO[:, k, :], in0=X[:, k, :], scalar=gain[:, k:k + 1],
                                         in1=HHI[:, k, :], op0=ALU.mult, op1=ALU.subtract).then_inc(h_lo, 1)

            def pre(L, s, tile=lambda k: None):
                for k in range(KT):
                    tile(k)
                    if k == 0:
                        dve.memset(SS[:], 0.0)
                    if k > 0:
                        low(L, s, k - 1)
                    if k > 1:
                        add_square(L, Q_PRE[s] + k - 2, SS[:])
                low(L, s, KT - 1)
                add_square(L, Q_PRE[s] + KT - 2, SS[:])
                add_square(L, Q_PRE[s] + KT - 1, SS[:])
                dve.wait_ge(pre_r, L * 3 + (s + 1))
                dve.memset(SS[:], 0.0)

            def down(L, s, c0, j0, per, k_outer=False):
                for m in range(KT):
                    c = c0 + 3 if k_outer and m < 4 else c0 + m * per + per - 1
                    if m == KT - 1:
                        dve.wait_ge(sq_done, L * LAYER_SQ + (Q_POST[s] + KT))
                    take(L, c, Y[:, m, :], bank[m % 4][:], jobs_r=False).then_inc(proj_free, 1)
                    if m < KT - 1:
                        add_square(L, Q_POST[s] + m, SS[:])
                dve.wait_ge(post_r, L * 3 + (s + 1))

            def residual(s, k):
                gain = cur[:, P_GAIN + (2 * s + 1) * KT:]
                dve.scalar_tensor_tensor(out=Y[:, k, :], in0=Y[:, k, :], scalar=gain[:, k:k + 1],
                                         in1=RP[:], op0=ALU.mult, op1=ALU.mult)
                dve.drain()
                dve.tensor_tensor(X[:, k, :], X[:, k, :], Y[:, k, :], ALU.add).then_inc(x_ready, 1)

            def ffn(L, s):
                c0, j0, c1, j1 = ((C_UP0, J_UP0, C_DOWN0, J_DOWN0), None, (C_UP1, J_UP1, C_DOWN1, J_DOWN1))[s]
                if s == 0:
                    pre(L, s)
                else:
                    pre(L, s, lambda k: residual(s - 1, k))

                def body(i, first):
                    for b in range(2):
                        n = (L * 2 + s // 2) * FT + i * 2 + (b + 1)
                        dve.drain()
                        take(L, c0 + (3 if first else 2 * b), TMP[:], bank[2 * b][:], i, 4).then_inc(proj_free, 1)
                        take(L, c0 + (3 if first else 2 * b + 1), UB[:], bank[2 * b + 1][:], i, 4).then_inc(proj_free, 1)
                        dve.drain()
                        dve.wait_ge(silu_ready, n)
                        dve.tensor_tensor(UB[:], UB[:], TMP[:], ALU.mult).then_inc(u_ready, 1)
                        dve.wait_ge(u_hi, n)
                        hi, lo = ((a[:, b, :] if first else a[:, bass.ds(i * 2 + b, 1), :].rearrange("p a n -> p (a n)"))
                                  for a in (UHI, ULO))
                        dve.tensor_tensor(lo, UB[:], hi, ALU.subtract).then_inc(u_lo, 1)
                body(0, True)
                with dve.Fori(1, FT // 2) as i:
                    body(i, False)
                down(L, s, c1, j1, DOWN_CHUNKS)
                if s == 2:
                    for k in range(KT):
                        residual(s, k)

            def mixer(L):
                pre(L, 1, lambda k: residual(0, k))
                for n, buf in enumerate((kT, vT)):
                    take(L, C_KV + 3, buf[:, CHUNK:], bank[2 + n][:]).then_inc(proj_free, 1)
                dve.memset(kT[:, 0:CHUNK], 0.0)
                dve.memset(vT[:, 0:CHUNK], 0.0).then_inc(pad_ready, 1)
                for buf in (KZ, SM):
                    dve.memset(buf[:], 0.0)
                dve.memset(RP[:], 0.0)
                chunked = lambda a: a.rearrange("p (c j) -> p c j", c=HCHUNKS)
                dve.wait_ge(setup_dma, 48)
                with dve.Fori(0, NT) as t:
                    it = L * NT + t
                    sink = cur[:, bass.ds(t + P_SINK, 1)]
                    lower, upper = lb[:, bass.ds(t, 1)], lb[:, bass.ds(t + NT, 1)]
                    for n in range(4):
                        take(L, C_GROUP0 + n, PROJ[:, n, :], bank[n][:], t, 4).then_inc(proj_free, 1)
                    dve.wait_ge(sig_ready, it + 1)
                    dve.tensor_scalar(SIGF, SIGF, upper, lower, ALU.mult, ALU.add)
                    dve.drain()
                    dve.tensor_scalar(SIGF, SIGF, FG_MIN, None, ALU.max).then_inc(fg_ready, 1)
                    dve.tensor_scalar(KK[:], SIGNF, upper, None, ALU.mult)
                    dve.tensor_tensor(PROJ[:, Q, :], PROJ[:, Q, :], SIGQ, ALU.mult)
                    dve.wait_ge(qk_full, it + 1)
                    bias_t = bias[:, bass.ds(t, 1), :]
                    dve.memset(Slog[:, 0, 0:CHUNK], NEG_INF)
                    for a, z, k0 in ((0, 1, CHUNK), (1, 4, 0), (4, 8, 0)):
                        src = bank[4 + a // 4][:].rearrange("p (n k) -> p n k", n=4)[:, a % 4:a % 4 + z - a, k0:]
                        dve.scalar_tensor_tensor(out=Slog[:, a:z, k0:], in0=src, scalar=HEAD_DIM ** -0.5,
                                                 in1=bias_t[:, :, k0:].to_broadcast([P, z - a, WINDOW - k0]),
                                                 op0=ALU.mult, op1=ALU.add)
                    dve.drain()
                    top = small[:, 0, :]
                    dve.tensor_reduce(top, Slog, AX_X, ALU.max)
                    dve.drain()
                    dve.tensor_scalar(top, top, sink, None, ALU.max)
                    dve.drain()
                    dve.tensor_scalar(Ssink, top, sink, -1.0, ALU.subtract, ALU.mult)
                    dve.tensor_tensor(Slog, Slog, top.unsqueeze(2).to_broadcast([P, 8, WINDOW]), ALU.subtract)\
                        .then_inc(logit_ready, 1)
                    dve.wait_ge(lf_ready, it + 1)
                    for c in range(HCHUNKS):
                        w = slice(c * P, c * P + P)
                        ins = dve.tensor_tensor_scan(BC[:, w], ones[:], LF[:, w], 0.0, ALU.mult, ALU.add)
                    ins.then_inc(bc_ready, 1)
                    dve.wait_ge(exp_ready, it + 1)
                    total, inverse = small[:, 1, :], small[:, 2, :]
                    dve.tensor_reduce(total, Slog, AX_X, ALU.add)
                    dve.drain()
                    dve.tensor_tensor(total, total, Ssink, ALU.add)
                    dve.drain()
                    dve.reciprocal(inverse, total)
                    dve.drain()
                    dve.tensor_tensor(Slog, Slog, inverse.unsqueeze(2).to_broadcast([P, 8, WINDOW]), ALU.mult)\
                        .then_inc(p_ready, 1)

                    def stage(n):
                        dve.wait_ge(decay, it * STAGES + (n + 1))
                        e, q = DD[:, n % DD_SLOTS, :], PROJ[:, Q, :]
                        if n == 0:
                            ins = dve.tensor_tensor(QB[:], q, e, ALU.mult)
                        elif n == 1:
                            ins = dve.tensor_tensor(KH[:], KK[:], e, ALU.mult)
                        elif n == STAGES - 1:
                            dve.sem_inc(held)
                            dve.drain()
                            dve.tensor_tensor(q, q, DD[:, 2, :], ALU.mult)
                            ins = dve.tensor_tensor(KK[:], KK[:], DD[:, 1, :], ALU.mult)
                        else:
                            l, m = n - 2, HALVES[n - 2]
                            halves = lambda a: a.rearrange("p (b u m) -> p b u m", u=2, m=m)
                            packed = QC[:, l, :, :].rearrange("p c j -> p (c j)").rearrange("p (b m) -> p b m", m=m)
                            dve.tensor_tensor(packed, halves(q)[:, :, 1, :], halves(e)[:, :, 1, :], ALU.mult)
                            ins = dve.tensor_tensor(halves(KZ[:, l, :])[:, :, 0, :], halves(KK[:])[:, :, 0, :],
                                                    halves(e)[:, :, 0, :], ALU.mult)
                        ins.then_inc(staged, 1)

                    def pick(n):
                        b = 4 + 2 * (n % 2)
                        dve.wait_ge(lv_full, it * SCORE_SETS + (n + 1))
                        dve.sem_inc(held)
                        for l in range(2 * n, min(2 * n + 2, NLEV)):
                            m = HALVES[l]
                            dve.drain()
                            mask = mask_sb[:, 64 * l:64 * l + 64].rearrange("p (b m) -> p b m", m=m)
                            for h in range(2):
                                at = (l - 2 * n) * 256
                                src = bank[b + h][:, at:at + 256].rearrange("p (c b m) -> p c b m", c=HCHUNKS, m=m)
                                dst = SM[:, h, :, :].rearrange("p c (b u m) -> p c b u m", u=2, m=m)[:, :, :, 1, :]
                                ins = dve.copy_predicated(dst, mask.unsqueeze(1).to_broadcast([P, HCHUNKS, 64 // m, m]), src)
                        if 2 * n >= NLEV:
                            dve.drain()
                            for h in range(2):
                                ins = dve.copy_predicated(SM[:, h, :, :], pair_sb.unsqueeze(1).to_broadcast([P, HCHUNKS, P]),
                                                          bank[b + h][:].rearrange("p (c j) -> p c j", c=HCHUNKS))
                        ins.then_inc(lv_used, 1)

                    for n in range(5):
                        stage(n)
                    dve.wait_ge(sq_done, L * LAYER_SQ + t + (Q_YA + 1))
                    dve.tensor_tensor(RP[:], RP[:], SQ[:, 0, :], ALU.add).then_inc(sq_free, 1)
                    dve.wait_ge(ds_full, it + 1)
                    dve.wait_ge(edec_ready, it + 1)
                    dve.tensor_copy(ST[:, 0, :], bank[7][:, 0:64])
                    for c in range(1, HCHUNKS - 1):
                        dve.drain()
                        ins = dve.scalar_tensor_tensor(out=ST[:, c, :], in0=ST[:, c - 1, :], scalar=edec[:, c:c + 1],
                                                       in1=bank[7][:, 64 * c:64 * c + 64], op0=ALU.mult, op1=ALU.add)
                    ins.then_inc(st_ready, 1)
                    stage(5)
                    pick(0)
                    stage(6)
                    stage(7)
                    pick(1)
                    stage(8)
                    pick(2)
                    pick(3)
                for n in range(NT):
                    take(L, C_GROUPS + 4 * (NT - 1) + n, G[:, n, :], bank[n][:]).then_inc(proj_free, 1)

                def z_low(k):
                    dve.wait_ge(z_hi, L * KT + (k + 1))
                    dve.tensor_tensor(HLO[:, k, :], Y[:, k, :], HHI[:, k, :], ALU.subtract).then_inc(z_lo, 1)
                dve.wait_ge(ya_r, L + 1)
                for k in range(KT):
                    if k == NT:
                        z_low(k - 1)
                    if k < NT:
                        dve.scalar_tensor_tensor(out=Y[:, k, :], in0=Y[:, k, :], scalar=cur[:, P_YA + k:P_YA + k + 1],
                                                 in1=RP[:], op0=ALU.mult, op1=ALU.mult).then_inc(z_ready, 1)
                    else:
                        n = k - NT
                        dve.wait_ge(yh_r, L * NT + (n + 1))
                        dve.scalar_tensor_tensor(out=Y[:, k, :], in0=Y[:, k, :], scalar=cur[:, P_YH + n:P_YH + n + 1],
                                                 in1=DD[:, n, :], op0=ALU.mult, op1=ALU.mult)
                        dve.wait_ge(g_sig, L * NT + (n + 1))
                        dve.tensor_tensor(G[:, n, :], G[:, n, :], GATE[:, n, :], ALU.mult)
                        dve.drain()
                        dve.tensor_tensor(Y[:, k, :], Y[:, k, :], G[:, n, :], ALU.mult).then_inc(z_ready, 1)
                    if k > 0 and k != NT:
                        z_low(k - 1)
                z_low(KT - 1)
                down(L, 1, C_OUT, J_OUT, 1, k_outer=True)

            dve.wait_ge(const_dma, 16 * 7)
            top = lbw[:, 4, :]
            dve.tensor_tensor(top, par[:, 0, P_LB:P_LB + NT], par[:, 1, P_LB:P_LB + NT], ALU.max)
            dve.drain()
            dve.tensor_tensor(lbw[:, 0, :], par[:, 0, P_LB:P_LB + NT], top, ALU.subtract)
            dve.tensor_tensor(lbw[:, 1, :], par[:, 1, P_LB:P_LB + NT], top, ALU.subtract).then_inc(setup, 1)
            for h in range(HEADS):
                ins = dve.tensor_scalar(oh_rel[:, h * RELS:h * RELS + RELS], oh_sb, rel_sb[:, h:h + 1], None, ALU.mult)
            ins.then_inc(setup, 1)
            dve.wait_ge(setup_act, 1)
            dve.tensor_tensor(lbw[:, 4, :], lbw[:, 2, :], lbw[:, 3, :], ALU.add)
            dve.drain()
            dve.reciprocal(lbw[:, 5, :], lbw[:, 4, :])
            dve.drain()
            dve.tensor_tensor(lbw[:, 0, :], lbw[:, 2, :], lbw[:, 5, :], ALU.mult)
            dve.tensor_tensor(lbw[:, 1, :], lbw[:, 3, :], lbw[:, 5, :], ALU.mult)
            dve.drain()
            dve.tensor_tensor(lb_all[:, 0, 0:NT], lbw[:, 0, :], lbw[:, 0, :], ALU.subtract)
            dve.tensor_tensor(lbw[:, 1, :], lbw[:, 0, :], lbw[:, 1, :], ALU.add)
            dve.drain()
            dve.tensor_tensor(lb_all[:, 1, 0:NT], lbw[:, 1, :], lbw[:, 0, :], ALU.subtract)
            dve.drain()
            dve.tensor_scalar(lb_all[:, :, NT:], lb_all[:, :, 0:NT], -1.0, 1.0, ALU.mult, ALU.add)
            dve.wait_ge(setup_pe, 1)
            for n in range(4):
                ins = dve.tensor_copy(relT[:, 2 * n * RELS:2 * (n + 1) * RELS], bank[n][0:CHUNK, 0:2 * RELS])
            ins.then_inc(setup, 1)
            dve.wait_ge(const_ready, 1)
            dve.memset(TMP[:, 0:1], 0.0).then_inc(x_ready, KT)
            dve.drain()
            with dve.Fori(0, DEPTH) as L:
                dve.tensor_copy(cur[:], par[:, bass.ds(L, 1), :].rearrange("p a n -> p (a n)"))
                dve.tensor_copy(lb[:], lb_all[:, bass.ds(L, 1), :].rearrange("p a n -> p (a n)"))
                dve.drain()
                for s in (0, 2):
                    g = cur[:, P_GAIN + (2 * s + 1) * KT:P_GAIN + (2 * s + 2) * KT]
                    ins = dve.tensor_scalar(g, g, 0.5, None, ALU.mult)
                ins.then_inc(cur_ready, 1)
                ffn(L, 0)
                mixer(L)
                ffn(L, 2)


ACT_WIDTH = HEADS * HEAD_DIM
YH_BANK = [5, 6, 7, 4]


def weight_stream(w_ffn_in, w_ffn_out, w_in, w_out):
    def columns(w):
        k, n = w.shape[0] // P, w.shape[1] // P
        return w.reshape(k, P, n, P).transpose(2, 1, 0, 3)

    def chunks(tiles, sizes):
        n = tiles.shape[0]
        out = np.zeros((n, len(sizes), P, TILES, P), tiles.dtype)
        at = 0
        for j, size in enumerate(sizes):
            out[:, j, :, :size, :] = tiles[:, :, at:at + size, :]
            at += size
        return out.reshape(n * len(sizes), P, CW)

    def k_outer(tiles):
        return tiles.reshape(4, P, 4, 2, P).transpose(2, 1, 3, 0, 4).reshape(4, P, CW)

    def paired(w, axis):
        order = [t + NT * half for t in range(NT) for half in range(2)]
        shape = w.shape
        w = w.reshape(shape[:axis] + (HEADS, HEAD_DIM) + shape[axis + 1:])
        return np.take(w, order, axis=axis).reshape(shape)

    width, kv = HEADS * HEAD_DIM, 2 * HEAD_DIM
    parts = []
    for layer in range(DEPTH):
        def ffn(j):
            gate_up = columns(w_ffn_in[layer, j])
            order = [n for m in range(FT) for n in (m, FT + m)]
            parts.append(k_outer(gate_up[order[:4]]))
            parts.append(chunks(gate_up[order[4:]], [TILES]))
            sizes = [min(TILES, FT - n * TILES) for n in range(DOWN_CHUNKS)]
            parts.append(chunks(columns(w_ffn_out[layer, j]), sizes))

        ffn(0)
        w = w_in[layer]
        at = 0
        cut = []
        for size in (width, kv, kv, width, width, width, width):
            cut.append(w[:, at:at + size])
            at += size
        qa, ka, va, qh, fh, ih, gh = cut
        group = [columns(a) for a in (fh, paired(qa, 1), qh, ih)]
        parts.append(k_outer(np.stack([group[F][0], group[QA][0], columns(ka)[0], columns(va)[0]])))
        parts.append(chunks(np.stack([group[Q][0], group[I][0]]), [4, 4]))
        parts.append(chunks(np.stack([g[1:] for g in group], axis=1).reshape((-1,) + group[0].shape[1:]), [TILES]))
        parts.append(chunks(columns(gh), [TILES]))
        rows = np.concatenate([paired(w_out[layer, :width], 0), w_out[layer, width:]], axis=0)
        parts.append(k_outer(columns(rows)[:4]))
        parts.append(chunks(columns(rows)[4:], [TILES]))
        ffn(1)
    out = np.concatenate(parts, axis=0)
    assert out.shape == (DEPTH * LAYER_CHUNKS, P, CW)
    return out


def kernel(x, norm_gains, w_ffn_in, w_ffn_out, w_in, w_out, attn_sinks, attn_out_gain,
           rel_bias, hgrn_lb_logits, hgrn_norm_gain):
    import concourse.bacc as bacc
    from concourse.bass_utils import run_bass_kernel_spmd

    def by_partition(a):
        a = np.asarray(a)
        return a.reshape(DEPTH, -1, P).transpose(2, 0, 1)

    ya_gain = np.asarray(attn_out_gain).reshape(DEPTH, 2, NT, HEAD_DIM).transpose(0, 2, 1, 3).reshape(DEPTH, -1)
    params = np.zeros((P, DEPTH, P_COLS), np.float32)
    params[:, :, P_GAIN:P_YA] = by_partition(norm_gains)
    params[:, :, P_YA:P_YH] = by_partition(ya_gain)
    params[:, :, P_YH:P_SINK] = by_partition(hgrn_norm_gain)
    params[:, :, P_LB:P_COLS] = by_partition(hgrn_lb_logits)
    arrays = {
        "xT": np.ascontiguousarray(np.asarray(x)[0].reshape(SEQ, KT, P).transpose(2, 1, 0)),
        "stream": weight_stream(*(np.asarray(w) for w in (w_ffn_in, w_ffn_out, w_in, w_out))),
        "params": params,
        "sinks": np.ascontiguousarray(attn_sinks),
        "rel_bias": np.ascontiguousarray(rel_bias),
        "one_hot": t5_bucket_one_hot(),
        "masks": np.concatenate([level_masks(), pair_mask()], axis=1),
    }
    nc = bacc.Bacc("TRN2", target_bir_lowering=False, num_devices=1)
    args = [nc.dram_tensor(n, a.shape, mybir.dt.from_np(a.dtype), kind="ExternalInput").ap() for n, a in arrays.items()]
    out = nc.dram_tensor("yT", (P, KT, SEQ), F32, kind="ExternalOutput").ap()
    build_program(nc, *args, out)
    result = run_bass_kernel_spmd(nc, [arrays], core_ids=[0])
    yT = result.results[0]["yT"]
    return yT.transpose(2, 1, 0).reshape(1, SEQ, D_MODEL)
```

```python
from contextlib import ExitStack

import numpy as np

import concourse.bass as bass
from concourse import mybir
from concourse.alu_op_type import AluOpType as ALU

ACT = mybir.ActivationFunctionType
F32 = mybir.dt.float32
F32R = mybir.dt.float32r
U32 = mybir.dt.uint32
AX_X = mybir.AxisListType.X

P = 128
DEPTH, SEQ, D_MODEL, D_FF = 2, 512, 1024, 2816
HEADS, HEAD_DIM, CHUNK = 8, 64, 64
WINDOW = 2 * CHUNK
KT = D_MODEL // P
FT = D_FF // P
NT = HEADS // 2
BUCKETS, REL_MAX_DIST = 32, 128
NORM_EPS = 1e-6
NEG_INF = -1e30
FG_MIN = 2.0 ** -63

HCHUNKS = SEQ // P
HALVES = [64, 32, 16, 8, 4, 2]
NLEV = len(HALVES)
STAGES = NLEV + 3
DD_SLOTS = 4
QC_SLOTS = 4
F, QA, Q, I = range(4)
SCORE_SETS = NLEV // 2 + 1
RELS = WINDOW + CHUNK - 1

RAW_SLOTS, SPLIT_SLOTS, PROJ_BANKS, SQ_SLOTS = 4, 2, 4, 2
TILES = 8
CW = TILES * P
DOWN_CHUNKS = -(-FT // TILES)
FFN_IN, FFN_OUT = 2 * FT, KT * DOWN_CHUNKS
KV_CHUNKS = 4
C_UP0 = 0
C_DOWN0 = C_UP0 + FFN_IN
C_KV = C_DOWN0 + FFN_OUT
C_GROUP0 = C_KV + KV_CHUNKS
C_GROUPS = C_GROUP0 + 4
C_OUT = C_GROUPS + 4 * NT
C_UP1 = C_OUT + KT
C_DOWN1 = C_UP1 + FFN_IN
LAYER_CHUNKS = C_DOWN1 + FFN_OUT
assert all(c % RAW_SLOTS == 0 for c in (C_DOWN0, C_KV, C_GROUP0, C_OUT, C_UP1, C_DOWN1, LAYER_CHUNKS))

J_UP0 = 0
J_DOWN0 = J_UP0 + FFN_IN
J_KV = J_DOWN0 + KT
J_GROUP0 = J_KV + 2
J_GROUPS = J_GROUP0 + 4
J_OUT = J_GROUPS + 4 * NT
J_UP1 = J_OUT + KT
J_DOWN1 = J_UP1 + FFN_IN
LAYER_JOBS = J_DOWN1 + KT

HALF = SEQ // 2
HALVES_OF = [slice(0, HALF), slice(HALF, SEQ)]
SPLIT_TILES = 2
INPUT_PARTS = [(k, w) for w in HALVES_OF for k in range(SPLIT_TILES)] + \
    [(k, slice(0, SEQ)) for k in range(SPLIT_TILES, KT)]
XT = len(INPUT_PARTS)
POOL_TILES = [3, 4, 5, 6]
LAST_ORDER = [k for k in range(KT) if k not in POOL_TILES] + POOL_TILES

Q_PRE = [0, 16, 36]
Q_YA = 24
Q_POST = [8, 28, 44]
LAYER_SQ = 52
POOL_SQ = 5

P_GAIN, P_YA, P_YH, P_LB, P_SINK = 0, 6 * KT, 6 * KT + NT, 6 * KT + 2 * NT, 6 * KT + 3 * NT
P_COLS = P_SINK + NT


def t5_bucket_one_hot():
    rel = np.arange(RELS) - (WINDOW - 1)
    nb = BUCKETS // 2
    n, exact = np.abs(rel), nb // 2
    large = exact + (np.log(np.maximum(n, 1) / exact) / np.log(REL_MAX_DIST / exact) * (nb - exact)).astype(np.int32)
    bucket = (rel > 0).astype(np.int32) * nb + np.where(n < exact, n, np.minimum(large, nb - 1))
    return (bucket[None, :] == np.arange(BUCKETS)[:, None]).astype(np.float32)


def level_masks():
    out = np.zeros((P, NLEV, P // 2), np.uint32)
    key = np.arange(P)
    for n, m in enumerate(HALVES):
        for q in range(P // 2):
            out[:, n, q] = (key // (2 * m) == q // m) & (key % (2 * m) < m)
    return out.reshape(P, -1)


def pair_mask():
    key, query = np.arange(P)[:, None], np.arange(P)[None, :]
    return ((key // 2 == query // 2) & (key <= query)).astype(np.uint32)


def build_program(nc, xT, stream, params, sinks, rel_bias, one_hot, masks, out):
    with ExitStack() as ctx:
        def sb(name, shape, dt=F32, scope=ctx):
            return scope.enter_context(nc.sbuf_tensor(name, shape, dt))

        def sem(name):
            return ctx.enter_context(nc.semaphore(name))

        X = sb("X", [P, KT, SEQ])
        HHI = sb("HHI", [P, KT, SEQ], F32R)
        HLO = sb("HLO", [P, KT, SEQ], F32R)
        RAW = sb("RAW", [P, RAW_SLOTS, CW])
        WHI = sb("WHI", [P, SPLIT_SLOTS, CW], F32R)
        WLO = sb("WLO", [P, SPLIT_SLOTS, CW], F32R)
        Y = sb("Y", [P, KT, SEQ])
        R = sb("R", [P, SEQ])
        RP = sb("RP", [P, SEQ])
        SS = sb("SS", [P, SEQ])
        SQ = sb("SQ", [P, SQ_SLOTS, SEQ])
        TMP = sb("TMP", [P, SEQ])
        UB = sb("UB", [P, SEQ])
        ones = sb("ones", [P, P])
        block_ones = sb("block_ones", [P, P])
        ident = sb("ident", [P, P])
        par = sb("par", [P, DEPTH, P_COLS])
        cur = sb("cur", [P, P_COLS])
        bias = sb("bias", [P, NT, WINDOW])
        mask_sb = sb("mask_sb", [P, NLEV * (P // 2) + P], U32)
        pair_sb = mask_sb[:, NLEV * (P // 2):]
        eps = sb("eps", [P, 1])
        lbw = sb("lbw", [P, 6, NT])
        lb_all = sb("lb_all", [P, DEPTH, 2 * NT])
        lb = sb("lb", [P, 2 * NT])
        out_gain = sb("out_gain", [P, KT])
        small = sb("small", [P, 3, 8])
        edec = sb("edec", [P, HCHUNKS])

        with ExitStack() as ffn_scope:
            UHI = sb("UHI", [P, FT, SEQ], F32R, ffn_scope)
            ULO = sb("ULO", [P, FT, SEQ], F32R, ffn_scope)
        kT = sb("kT", [P, CHUNK + SEQ])
        vT = sb("vT", [P, CHUNK + SEQ])
        vwin = sb("vwin", [P, 8, P])
        KZ = sb("KZ", [P, NLEV, SEQ])
        QC = sb("QC", [P, QC_SLOTS, HCHUNKS, 2, P // 2])
        SM = sb("SM", [P, HCHUNKS, 2, P])
        S = sb("S", [P, 8 * WINDOW + 8])
        PT = sb("PT", [P, 8, P])
        PROJ = sb("PROJ", [P, 4, SEQ])
        GATE = sb("GATE", [P, 4, SEQ])
        BC = sb("BC", [P, SEQ])
        KK = sb("KK", [P, SEQ])
        DD = sb("DD", [P, DD_SLOTS, SEQ])
        QB = sb("QB", [P, SEQ])
        KH = sb("KH", [P, SEQ])
        KHT = sb("KHT", [P, HCHUNKS, P])
        VTOK = sb("VTOK", [P, HCHUNKS, P])
        ST = sb("ST", [P, HCHUNKS - 1, HEAD_DIM])
        YR = sb("YR", [P, NT, SEQ])
        YSQ = sb("YSQ", [P, SEQ])
        Slog = S[:, 0:8 * WINDOW].rearrange("p (n k) -> p n k", n=8)
        Ssink = S[:, 8 * WINDOW:]
        SIGF, SIGNF, SIGQ, LF = (GATE[:, n, :] for n in range(4))

        bank = [ctx.enter_context(nc.psum_tensor(f"bank{n}", [P, SEQ], F32)) for n in range(8)]

        rel_scratch = nc.dram_tensor("rel_scratch", (CHUNK * HEADS * RELS,), F32, kind="Internal").ap()
        rel_rows = KZ[0:HEADS, 0, 0:RELS]
        oh_sb = QC[0:BUCKETS, 0, :, :, :].rearrange("p a b c -> p (a b c)")[:, 0:RELS]
        rel_sb = small[0:BUCKETS, 0, :]

        w_dma = [sem(f"w_dma{n}") for n in range(RAW_SLOTS)]
        w_hi = sem("w_hi")
        w_split = sem("w_split")
        w_used = sem("w_used")
        proj_free = sem("proj_free")
        sq_done = sem("sq_done")
        sq_free = sem("sq_free")
        const_dma = sem("const_dma")
        mask_dma = sem("mask_dma")
        x_dma = [sem(f"x_dma{n}") for n in range(KT // 2)]
        const_ready = sem("const_ready")
        setup = sem("setup")
        setup_act = sem("setup_act")
        setup_pe = sem("setup_pe")
        setup_dma = sem("setup_dma")
        cur_ready = sem("cur_ready")
        x_ready = sem("x_ready")
        h_hi = sem("h_hi")
        h_lo = sem("h_lo")
        four_full = sem("four_full")
        half_full = sem("half_full")
        half_sq = sem("half_sq")
        half_sum = sem("half_sum")
        pre_sum = sem("pre_sum")
        pre_r = sem("pre_r")
        post_r = sem("post_r")
        silu_ready = sem("silu_ready")
        u_ready = sem("u_ready")
        u_hi = sem("u_hi")
        u_lo = sem("u_lo")
        pad_ready = sem("pad_ready")
        vwin_full = sem("vwin_full")
        vwin_ready = sem("vwin_ready")
        qk_full = sem("qk_full")
        logit_ready = sem("logit_ready")
        exp_ready = sem("exp_ready")
        p_ready = sem("p_ready")
        pt_full = sem("pt_full")
        pt_ready = sem("pt_ready")
        pv_full = sem("pv_full")
        ya_ready = sem("ya_ready")
        sig_ready = sem("sig_ready")
        fg_ready = sem("fg_ready")
        lf_ready = sem("lf_ready")
        bc_ready = sem("bc_ready")
        edec_ready = sem("edec_ready")
        exponent = sem("exponent")
        decay = sem("decay")
        staged = sem("staged")
        vtok_full = sem("vtok_full")
        vtok_ready = sem("vtok_ready")
        kht_full = sem("kht_full")
        kht_ready = sem("kht_ready")
        ds_full = sem("ds_full")
        st_ready = sem("st_ready")
        lv_full = sem("lv_full")
        lv_used = sem("lv_used")
        o_full = sem("o_full")
        g_sig = sem("g_sig")
        ya_sum = sem("ya_sum")
        ya_r = sem("ya_r")
        yh_sq = sem("yh_sq")
        yh_sum = sem("yh_sum")
        yh_r = sem("yh_r")
        z_ready = sem("z_ready")
        z_hi = sem("z_hi")
        z_lo = sem("z_lo")
        last_scaled = sem("last_scaled")
        stored = sem("stored")
        held = sem("held")

        block = ctx.enter_context(nc.Block())

        @block.sync
        def _(sp):
            sp.dma_start(rel_sb, rel_bias).then_inc(const_dma, 16)
            sp.dma_start(oh_sb, one_hot).then_inc(const_dma, 16)
            sp.dma_start(par[:, :, 0:P_SINK], params).then_inc(const_dma, 16)
            for half in range(2):
                dst = par[half * 64:half * 64 + 64, :, P_SINK:]
                src = sinks[:, half * NT:half * NT + NT].unsqueeze(0).to_broadcast([64, DEPTH, NT])
                sp.dma_start(dst, src).then_inc(const_dma, 16)
            for n in range(RAW_SLOTS):
                sp.dma_start(X[:, 2 * n:2 * n + 2, :], xT[:, 2 * n:2 * n + 2, :]).then_inc(x_dma[n], 16)
                sp.dma_start(RAW[:, n, :], stream[n]).then_inc(w_dma[n], 16)
            sp.dma_start(mask_sb[:], masks).then_inc(mask_dma, 16)
            sp.wait_ge(setup, 2)
            sp.dma_start(rel_scratch.rearrange("(q h c) -> h q c", q=CHUNK, h=HEADS),
                         rel_rows.unsqueeze(1).to_broadcast([HEADS, CHUNK, RELS])).then_inc(setup_dma, 16)
            sp.wait_ge(setup_dma, 16)
            for half in range(2):
                base = half * NT * RELS + CHUNK - 1
                src = bass.AP(tensor=rel_scratch.tensor, offset=base,
                              ap=[[HEADS * RELS - 1, CHUNK], [RELS, NT], [1, WINDOW]])
                sp.dma_start(bias[half * 64:half * 64 + 64, :, :], src).then_inc(setup_dma, 16)
            with sp.Fori(1, DEPTH * LAYER_CHUNKS // RAW_SLOTS) as i:
                for n in range(RAW_SLOTS):
                    sp.wait_ge(w_split, i * RAW_SLOTS + (n + 1))
                    sp.dma_start(RAW[:, n, :], stream[i * RAW_SLOTS + n]).then_inc(w_dma[n], 16)
            for n, k in enumerate(LAST_ORDER):
                sp.wait_ge(x_ready, XT * (3 * DEPTH) + SPLIT_TILES + n + 1)
                sp.dma_start(out[:, k, :], X[:, k, :]).then_inc(stored, 16)
            sp.wait_ge(stored, 16 * KT)

        @block.gpsimd
        def _(pool):
            pool.memset(eps[:], NORM_EPS)
            pool.memset(ones[:], 1.0)
            pool.memset(block_ones[:], 0.0)
            pool.memset(ident[:], 0.0)
            pool.drain()
            for h in range(2):
                pool.memset(block_ones[64 * h:64 * h + 64, 64 * h:64 * h + 64], 1.0)
                pool.drain()
            pool.affine_select(out=ident[:], in_=ident[:], compare_op=ALU.not_equal, fill=1.0, base=0,
                               pattern=[[-1, P]], channel_multiplier=1)
            pool.drain()
            pool.memset(small[:, 2, 0:1], 0.0).then_inc(w_split, RAW_SLOTS)
            pool.memset(small[:, 2, 1:2], 0.0).then_inc(w_used, SPLIT_SLOTS)
            pool.memset(small[:, 2, 2:3], 0.0).then_inc(proj_free, PROJ_BANKS - 1)
            pool.memset(small[:, 2, 6:7], 0.0).then_inc(post_r, 2)
            pool.memset(small[:, 2, 3:4], 0.0).then_inc(sq_free, SQ_SLOTS)
            pool.memset(small[:, 2, 5:6], 0.0).then_inc(yh_r, 1)
            pool.memset(small[:, 2, 4:5], 0.0).then_inc(const_ready, 1)
            pool.memset(Y[:, KT // 2:, :], 0.0).then_inc(const_ready, 1)

            def split_lo(L, c, i=0, per=0, cols=CW):
                n = c % RAW_SLOTS
                pool.wait_ge(w_hi, L * LAYER_CHUNKS + i * per + (c + 1))
                pool.tensor_tensor(WLO[:, n % 2, 0:cols], RAW[:, n, 0:cols], WHI[:, n % 2, 0:cols], ALU.subtract)\
                    .then_inc(w_split, 1)

            def exponents(n, it):
                if n >= DD_SLOTS:
                    pool.wait_ge(staged, it * STAGES + (n - DD_SLOTS + 1))
                dst = DD[:, n % DD_SLOTS, :]
                if n == 1:
                    chunked = lambda a: a.rearrange("p (c j) -> p c j", c=HCHUNKS)
                    ins = pool.tensor_tensor(chunked(dst), chunked(BC[:]),
                                             chunked(BC[:])[:, :, P - 1:P].to_broadcast([P, HCHUNKS, P]), ALU.subtract)
                else:
                    m = HALVES[n - 2] if n < STAGES - 1 else 1
                    blocks = BC[:].rearrange("p (b j) -> p b j", j=2 * m)
                    ins = pool.tensor_tensor(dst.rearrange("p (b j) -> p b j", j=2 * m), blocks,
                                             blocks[:, :, m - 1:m].to_broadcast([P, SEQ // (2 * m), 2 * m]), ALU.subtract)
                ins.then_inc(exponent, 1)

            def pre(L, s, c0):
                split_lo(L, c0)
                split_lo(L, c0 + 1)
                for k in range(1, POOL_SQ):
                    if k > 1:
                        pool.drain()
                    pool.wait_ge(sq_done, L * LAYER_SQ + (Q_PRE[s] + k + 1))
                    if k == 1:
                        pool.tensor_tensor(SS[:], SQ[:, 0, :], SQ[:, 1, :], ALU.add).then_inc(sq_free, 2)
                    else:
                        pool.tensor_tensor(SS[:], SS[:], SQ[:, k % 2, :], ALU.add).then_inc(sq_free, 1)
                    if k in (2, 4):
                        split_lo(L, c0 + k // 2 + 1)

            def split_rest(L, c0, c1):
                with pool.Fori(0, (c1 - c0) // RAW_SLOTS) as i:
                    for n in range(RAW_SLOTS):
                        split_lo(L, c0 + n, i, RAW_SLOTS)

            with pool.Fori(0, DEPTH) as L:
                pre(L, 0, C_UP0)
                split_rest(L, C_UP0 + 4, C_KV)
                pre(L, 1, C_KV)
                for c in range(C_GROUP0, C_GROUPS + 2):
                    split_lo(L, c, cols=CW // 2 if c < C_GROUPS else CW)
                with pool.Fori(0, NT) as t:
                    it = L * NT + t
                    split_lo(L, C_GROUPS + 2, t, 4)
                    pool.wait_ge(bc_ready, it + 1)
                    for n in range(1, 6):
                        exponents(n, it)
                    split_lo(L, C_GROUPS + 3, t, 4)
                    for n in range(6, STAGES):
                        exponents(n, it)
                    pool.wait_ge(sq_done, L * LAYER_SQ + t + (Q_YA + 1))
                    pool.tensor_tensor(RP[:], RP[:], SQ[:, 0, :], ALU.add).then_inc(sq_free, 1)
                    split_lo(L, C_GROUPS + 4, t, 4)
                    split_lo(L, C_GROUPS + 5, t, 4)
                for c in range(C_OUT + 2, C_UP1):
                    split_lo(L, c)
                pre(L, 2, C_UP1)
                split_rest(L, C_UP1 + 4, LAYER_CHUNKS)
            pool.wait_ge(post_r, (3 * DEPTH + 1) * 2)
            for k in POOL_TILES:
                pool.tensor_tensor(Y[:, k, :], Y[:, k, :], RP[:], ALU.mult).then_inc(last_scaled, 1)

        @block.scalar
        def _(act):
            def split_hi(L, c, i=0, per=0, cols=CW):
                n = c % RAW_SLOTS
                assert per % RAW_SLOTS == 0
                act.wait_ge(w_dma[n], (L * (LAYER_CHUNKS // RAW_SLOTS) + i * (per // RAW_SLOTS) + (c // RAW_SLOTS + 1)) * 16)
                act.wait_ge(w_used, L * LAYER_CHUNKS + i * per + (c + 1))
                act.activation(WHI[:, n % 2, 0:cols], RAW[:, n, 0:cols], ACT.Copy).then_inc(w_hi, 1)

            def square(L, q, src):
                act.wait_ge(sq_free, L * LAYER_SQ + (q + 1))
                act.activation(SQ[:, q % 2, :], src, ACT.Square).then_inc(sq_done, 1)

            def rsqrt_mean(dst, src, count):
                act.activation(dst, src, ACT.Ln, scale=1.0 / count, bias=eps[:, 0:1])
                act.drain()
                return act.activation(dst, dst, ACT.Exp, scale=-0.5)

            def high(L, s, p):
                k, w = INPUT_PARTS[p]
                act.wait_ge(x_ready, (L * 3 + s) * XT + (p + 1))
                act.activation(HHI[:, k, w], X[:, k, w], ACT.Copy,
                               scale=cur[:, P_GAIN + 2 * s * KT:][:, k:k + 1]).then_inc(h_hi, 1)

            def pre(L, s, c0, cols=CW):
                if s == 0:
                    split_hi(L, c0)
                    act.wait_ge(cur_ready, L + 1)
                    for p in range(2 * SPLIT_TILES):
                        high(L, s, p)
                        if p == 0:
                            split_hi(L, c0 + 1)
                squared = 0
                for k in range(SPLIT_TILES, KT):
                    high(L, s, k + SPLIT_TILES)
                    for _ in range(min(2, k - squared)):
                        square(L, Q_PRE[s] + squared, X[:, squared, :])
                        squared += 1
                    if k in (3, 5):
                        split_hi(L, c0 + (k + 1) // 2)
                square(L, Q_PRE[s] + KT - 1, X[:, KT - 1, :])
                split_hi(L, c0 + 4, cols=cols)
                act.wait_ge(pre_sum, L * 3 + (s + 1))
                rsqrt_mean(R[:], bank[4][:], D_MODEL).then_inc(pre_r, 1)

            def down(L, s, c0, j0, per, k_outer=False):
                def body(i, last):
                    for b in range(4):
                        for n in range(per):
                            if k_outer and i == 0:
                                if b == 0:
                                    split_hi(L, c0 + 5)
                            elif not (last and b == 3 and n >= per - (1 if s < 2 else 2)):
                                split_hi(L, c0 + b * per + n + 2, i, 4 * per)
                        q = Q_POST[s] + b
                        if not (last and b == 3):
                            act.wait_ge(proj_free, L * LAYER_JOBS + i * 4 + (j0 + b + 1 + PROJ_BANKS))
                            act.wait_ge(sq_free, L * LAYER_SQ + i * 4 + (q + 1))
                            act.activation(SQ[:, q % 2, :], Y[:, i * 4 + b, :], ACT.Square).then_inc(sq_done, 1)
                body(0, False)
                body(1, True)
                q = Q_POST[s] + KT - 1
                first, second = HALVES_OF
                act.wait_ge(half_full, L * 3 + (s + 1))
                act.wait_ge(sq_free, L * LAYER_SQ + (q + 1))
                act.activation(SQ[:, q % 2, first], bank[5][:, 0:HALF], ACT.Square).then_inc(half_sq, 1)
                act.wait_ge(half_sum, L * 3 + (s + 1))
                rsqrt_mean(RP[:, first], bank[4][:, 0:HALF], D_MODEL).then_inc(post_r, 1)
                if s < 2:
                    high(L, s + 1, 0)
                act.wait_ge(w_used, L * LAYER_CHUNKS + (c0 + KT * per + SPLIT_SLOTS))
                act.activation(SQ[:, q % 2, second], bank[6][:, 0:HALF], ACT.Square).then_inc(sq_done, 1)
                if s < 2:
                    split_hi(L, c0 + KT * per + 1)
                    for p in range(1, SPLIT_TILES):
                        high(L, s + 1, p)
                act.wait_ge(sq_free, L * LAYER_SQ + (q + 1 + SQ_SLOTS))
                rsqrt_mean(RP[:, second], bank[7][:, 0:HALF], D_MODEL).then_inc(post_r, 1)
                if s < 2:
                    for p in range(SPLIT_TILES, 2 * SPLIT_TILES):
                        high(L, s + 1, p)

            def ffn(L, s):
                c0, j0, c1, j1 = ((C_UP0, J_UP0, C_DOWN0, J_DOWN0), None, (C_UP1, J_UP1, C_DOWN1, J_DOWN1))[s]
                f = s // 2
                act.preload_act_table_set("natural_log_exp_and_others")
                pre(L, s, c0)
                act.preload_act_table_set("silu_and_others")

                def body(i, first):
                    for b in range(2):
                        n = (L * 2 + f) * FT + i * 2 + (b + 1)
                        if not first:
                            split_hi(L, c0 + 2 * b + 2, i, 4)
                            split_hi(L, c0 + 2 * b + 3, i, 4)
                        elif b == 0:
                            split_hi(L, c0 + 5)
                        act.wait_ge(proj_free, L * LAYER_JOBS + i * 4 + (j0 + 2 * b + 1 + PROJ_BANKS))
                        act.activation(TMP[:], TMP[:], ACT.Silu).then_inc(silu_ready, 1)
                        act.wait_ge(u_ready, n)
                        if first and b == 0:
                            act.wait_ge(setup_dma, 48)
                        u = UHI[:, b, :] if first else UHI[:, bass.ds(i * 2 + b, 1), :].rearrange("p a n -> p (a n)")
                        act.activation(u, UB[:], ACT.Copy).then_inc(u_hi, 1)
                body(0, True)
                with act.Fori(1, FT // 2) as i:
                    body(i, False)
                act.preload_act_table_set("natural_log_exp_and_others")
                down(L, s, c1, j1, DOWN_CHUNKS)

            def mixer(L):
                pre(L, 1, C_KV, CW // 2)
                split_hi(L, C_KV + 5, cols=CW // 2)
                for c in range(C_GROUP0 + 2, C_GROUPS + 2):
                    split_hi(L, c, cols=CW // 2 if c < C_GROUPS else CW)
                for half in range(2):
                    act.wait_ge(vwin_full, L * 2 + (half + 1))
                    act.activation(vwin[:, 4 * half:4 * half + 4, :].rearrange("p a b -> p (a b)"), bank[6 + half][:],
                                   ACT.Copy).then_inc(vwin_ready, 1)
                with act.Fori(0, NT) as t:
                    it = L * NT + t

                    def ahead(n):
                        split_hi(L, C_GROUPS + n + 2, t, 4)

                    def decays(n):
                        dst = DD[:, n % DD_SLOTS, :]
                        if n > 0:
                            act.wait_ge(exponent, it * (STAGES - 1) + n)
                        if n == 0:
                            ins = act.activation(dst, BC[:], ACT.Exp)
                        elif n == 1:
                            ins = act.activation(dst, dst, ACT.Exp, scale=-1.0)
                        elif n == STAGES - 1:
                            act.wait_ge(staged, it * STAGES + (STAGES - 2))
                            act.activation(DD[:, 1, :], dst, ACT.Exp, scale=-1.0)
                            ins = act.activation(DD[:, 2, :], dst, ACT.Exp)
                        else:
                            m = HALVES[n - 2]
                            dst = dst.rearrange("p (b u m) -> p b u m", u=2, m=m)
                            act.activation(dst[:, :, 0, :], dst[:, :, 0, :], ACT.Exp, scale=-1.0)
                            ins = act.activation(dst[:, :, 1, :], dst[:, :, 1, :], ACT.Exp)
                        ins.then_inc(decay, 1)

                    act.preload_act_table_set("sigmoid_and_others")
                    act.wait_ge(proj_free, L * LAYER_JOBS + t * 4 + (J_GROUP0 + 3 + PROJ_BANKS))
                    act.activation(SIGF, PROJ[:, F, :], ACT.Sigmoid)
                    act.activation(SIGNF, PROJ[:, F, :], ACT.Sigmoid, scale=-1.0)
                    act.activation(SIGQ, PROJ[:, Q, :], ACT.Sigmoid).then_inc(sig_ready, 1)
                    act.preload_act_table_set("natural_log_exp_and_others")
                    act.wait_ge(fg_ready, it + 1)
                    act.activation(LF, SIGF, ACT.Ln).then_inc(lf_ready, 1)
                    ahead(0)
                    act.wait_ge(logit_ready, it + 1)
                    act.activation(S[:], S[:], ACT.Exp).then_inc(exp_ready, 1)
                    act.wait_ge(bc_ready, it + 1)
                    act.activation(edec[:], BC[:].rearrange("p (c j) -> p c j", c=HCHUNKS)[:, :, P - 1], ACT.Exp)\
                        .then_inc(edec_ready, 1)
                    for n in range(3):
                        decays(n)
                    for half in range(2):
                        act.wait_ge(pt_full, it * 2 + (half + 1))
                        act.activation(PT[:, 4 * half:4 * half + 4, :].rearrange("p a b -> p (a b)"),
                                       bank[6 + half][:], ACT.Copy).then_inc(pt_ready, 1)
                    act.wait_ge(vtok_full, it + 1)
                    act.activation(VTOK[:].rearrange("p a b -> p (a b)"), bank[5][:], ACT.Copy).then_inc(vtok_ready, 1)
                    ahead(1)
                    decays(3)
                    act.wait_ge(pv_full, it + 1)
                    act.wait_ge(sq_free, L * LAYER_SQ + t + (Q_YA + 2))
                    act.activation(SQ[:, 0, :], bank[4][:], ACT.Square).then_inc(sq_done, 1)
                    act.activation(Y[:, bass.ds(t, 1), :].rearrange("p a n -> p (a n)"), bank[4][:], ACT.Copy)\
                        .then_inc(ya_ready, 1)
                    act.wait_ge(kht_full, it + 1)
                    act.activation(KHT[:].rearrange("p a b -> p (a b)"), bank[6][:], ACT.Copy).then_inc(kht_ready, 1)
                    for n in range(4, STAGES):
                        decays(n)
                    ahead(2)
                    act.wait_ge(o_full, it + 1)
                    act.activation(YSQ[:], bank[6][:], ACT.Square).then_inc(yh_sq, 1)
                    act.activation(Y[:, bass.ds(t + NT, 1), :].rearrange("p a n -> p (a n)"), bank[6][:], ACT.Copy)
                    ahead(3)
                    act.wait_ge(yh_sum, it + 1)
                    rsqrt_mean(YR[:, bass.ds(t, 1), :].rearrange("p a n -> p (a n)"), bank[7][:], HEAD_DIM).then_inc(yh_r, 1)
                def z_high(k):
                    act.wait_ge(z_ready, L * KT + (k + 1))
                    act.activation(HHI[:, k, :], Y[:, k, :], ACT.Copy).then_inc(z_hi, 1)

                act.wait_ge(ya_sum, L + 1)
                rsqrt_mean(RP[:], bank[4][:], ACT_WIDTH).then_inc(ya_r, 1)
                for k in range(NT):
                    z_high(k)
                    if k == 1:
                        act.preload_act_table_set("sigmoid_and_others")
                for k in range(NT):
                    act.wait_ge(proj_free, L * LAYER_JOBS + (J_OUT + PROJ_BANKS))
                    act.activation(GATE[:, k, :], PROJ[:, k, :], ACT.Sigmoid).then_inc(g_sig, 1)
                split_hi(L, C_OUT + 2)
                for k in range(NT, KT):
                    z_high(k)
                    if k == 5:
                        split_hi(L, C_OUT + 3)
                split_hi(L, C_OUT + 4)
                act.preload_act_table_set("natural_log_exp_and_others")
                down(L, 1, C_OUT, J_OUT, 1, k_outer=True)

            act.preload_act_table_set("natural_log_exp_and_others")
            act.wait_ge(setup, 1)
            act.activation(lbw[:, 2:4, :], lbw[:, 0:2, :], ACT.Exp).then_inc(setup_act, 1)
            with act.Fori(0, DEPTH) as L:
                ffn(L, 0)
                mixer(L)
                ffn(L, 2)

        @block.tensor
        def _(pe):
            def chunk(L, c, tiles, hi, lo, b, i=0, per=0, h_sem=None, h_value=None,
                      ready=True, done=True, signal=w_used, w=None, rhs_w=None):
                slot = c % 2
                assert per % 2 == 0
                if ready:
                    pe.wait_ge(w_split, L * LAYER_CHUNKS + i * per + (c + 1 + RAW_SLOTS))
                dst = bank[b][:] if w is None else bank[b][:, w]
                for at, k, first, last in tiles:
                    if h_sem is not None:
                        pe.wait_ge(h_sem, h_value + (k + 1))
                    lhs = slice(at * P, at * P + P)
                    rhs_hi, rhs_lo = (a[:, k, :] if rhs_w is None else a[:, k, rhs_w] for a in (hi, lo))
                    pe.matmul(dst, WHI[:, slot, lhs], rhs_hi, start=first, stop=False)
                    pe.matmul(dst, WHI[:, slot, lhs], rhs_lo, start=False, stop=False)
                    ins = pe.matmul(dst, WLO[:, slot, lhs], rhs_hi, start=False, stop=last)
                if done:
                    ins.then_inc(signal, 1)

            def bank_free(L, j, i=0, per=0, back=PROJ_BANKS):
                pe.wait_ge(proj_free, L * LAYER_JOBS + i * per + (j + 1 + PROJ_BANKS - back))

            FULL = [(k, k, k == 0, k == KT - 1) for k in range(KT)]

            def four(L, c0, h_sem, h_value, parts, order=(0, 1, 2, 3), between=None):
                for p, (k, w) in enumerate(parts):
                    c = k // 2
                    uses = [n for n, part in enumerate(parts) if part[0] // 2 == c]
                    pe.wait_ge(h_sem, h_value + (p + 1))
                    if p == uses[0]:
                        pe.sem_inc(held)
                    for j in order:
                        end = k == KT - 1 and j != order[-1]
                        chunk(L, c0 + c, [(k % 2 * 4 + j, k, p == 0, k == KT - 1)], HHI, HLO, j,
                              ready=p == uses[0] and j == order[0], done=end or p == uses[-1] and j == order[-1],
                              signal=four_full if end else w_used, w=w, rhs_w=w)
                    if between is not None:
                        between(k)

            def total(src, b, squares, done, lhs=None):
                pe.wait_ge(*squares)
                pe.matmul(bank[b][:], (lhs or ones)[:], src, start=True, stop=True).then_inc(done, 1)

            def pre_total(L, s):
                def at(k):
                    if k == KT - 2:
                        total(SS[:], 4, (sq_free, L * LAYER_SQ + (Q_PRE[s] + KT + SQ_SLOTS)), pre_sum)
                return at

            def down(L, s, c0, j0, width, hi, lo, h=None, k_outer=False):
                per = -(-width // TILES)
                for m in range(KT):
                    b = m % 4
                    if k_outer and m < 4:
                        if m == 0:
                            bank_free(L, j0 + 3)
                            four(L, c0, *h, [(k, slice(0, SEQ)) for k in range(KT)])
                        continue
                    bank_free(L, j0 + m)
                    for n in range(per):
                        tiles = [(k - n * TILES, k, k == 0, k == width - 1)
                                 for k in range(n * TILES, min(width, (n + 1) * TILES))]
                        c = c0 + m * per + n
                        if m < KT - 1:
                            first = h is not None and m == 0
                            chunk(L, c, tiles, hi, lo, b, h_sem=h[0] if first else None, h_value=h[1] if first else None)
                            continue
                        first, second = HALVES_OF
                        own = slice(0, HALF)
                        last_chunk = n == per - 1
                        chunk(L, c, tiles, hi, lo, 5, done=last_chunk, signal=half_full, w=own, rhs_w=first)
                        if last_chunk:
                            pe.wait_ge(sq_free, L * LAYER_SQ + (Q_POST[s] + KT - 1 + SQ_SLOTS))
                            pe.matmul(bank[4][:, own], ones[:], SS[:, first], start=True, stop=False)
                            pe.matmul(bank[7][:, own], ones[:], SS[:, second], start=True, stop=False)
                            pe.wait_ge(half_sq, L * 3 + (s + 1))
                            pe.matmul(bank[4][:, own], ones[:], SQ[:, (Q_POST[s] + KT - 1) % 2, first], start=False, stop=True)\
                                .then_inc(half_sum, 1)
                        chunk(L, c, tiles, hi, lo, 6, ready=False, w=own, rhs_w=second)
                pe.wait_ge(sq_done, L * LAYER_SQ + (Q_POST[s] + KT))
                pe.matmul(bank[7][:, 0:HALF], ones[:], SQ[:, (Q_POST[s] + KT - 1) % 2, HALVES_OF[1]], start=False, stop=True)\
                    .then_inc(sq_free, 1)

            def ffn(L, s):
                c0, j0, c1, j1 = ((C_UP0, J_UP0, C_DOWN0, J_DOWN0), None, (C_UP1, J_UP1, C_DOWN1, J_DOWN1))[s]
                bank_free(L, j0 + 2)
                four(L, c0, h_lo, (L * 3 + s) * XT, INPUT_PARTS, between=pre_total(L, s))
                with pe.Fori(1, FT // 2) as i:
                    for n in range(4):
                        bank_free(L, j0 + n, i, 4)
                        chunk(L, c0 + n, FULL, HHI, HLO, n, i, 4)
                down(L, s, c1, j1, FT, UHI, ULO, (u_lo, (L * 2 + s // 2) * FT))

            def mixer(L):
                bank_free(L, J_KV + 2)
                four(L, C_KV, h_lo, (L * 3 + 1) * XT, INPUT_PARTS, (2, 3, 0, 1), pre_total(L, 1))
                for n in range(4):
                    if n % 2 == 0:
                        bank_free(L, J_KV + 1 + n // 2, back=1)
                    ks = FULL[4 * (n % 2):4 * (n % 2) + 4]
                    chunk(L, C_GROUP0 + n, [(k - ks[0][1], k, first, last) for _, k, first, last in ks],
                          HHI, HLO, 2 + n // 2)
                pe.wait_ge(pad_ready, L + 1)
                for n in range(8):
                    ins = pe.transpose(bank[6 + n // 4][:, (n % 4) * P:(n % 4) * P + P], vT[:, CHUNK * n:CHUNK * n + P], ident[:])
                    if n % 4 == 3:
                        ins.then_inc(vwin_full, 1)
                with pe.Fori(0, NT) as t:
                    it = L * NT + t

                    def next_group(n, k0=0, k1=KT):
                        if k0 == 0:
                            bank_free(L, J_GROUPS + n, t, 4)
                        chunk(L, C_GROUPS + n, FULL[k0:k1], HHI, HLO, n, t, 4, ready=k0 == 0, done=k1 == KT)

                    def scores(l):
                        n = l // 2
                        b = 4 + 2 * (n % 2)
                        if l == 0:
                            pe.wait_ge(ya_ready, it + 1)
                        elif l == 2:
                            pe.wait_ge(st_ready, it + 1)
                        elif l % 2 == 0:
                            pe.wait_ge(lv_used, it * SCORE_SETS + (n - 1))
                        pe.wait_ge(staged, it * STAGES + (l + 3))
                        pe.sem_inc(held)
                        for c in range(HCHUNKS):
                            if l < NLEV:
                                keys = P // 2 if l == 0 else P
                                ins = pe.matmul(bank[b + l % 2][0:keys, c * P:c * P + P], KZ[:, l, c * P:c * P + keys],
                                                QC[:, l % QC_SLOTS, c, :, :].rearrange("p h q -> p (h q)"),
                                                start=True, stop=True)
                                continue
                            for h in range(2):
                                rows = slice(64 * h, 64 * h + 64)
                                ins = pe.matmul(bank[b + h][:, c * P:c * P + P], KK[rows, c * P:c * P + P],
                                                PROJ[rows, Q, c * P:c * P + P], start=True, stop=True)
                        if l % 2 == 1 or l == NLEV:
                            ins.then_inc(lv_full, 1)

                    next_group(0, 0, 4)
                    pe.wait_ge(proj_free, L * LAYER_JOBS + t * 4 + (J_GROUP0 + 2 + PROJ_BANKS))
                    pe.sem_inc(held)
                    for n in range(8):
                        for h in range(2):
                            rows = slice(64 * h, 64 * h + 64)
                            ins = pe.matmul(bank[4 + n // 4][rows, (n % 4) * P:(n % 4) * P + P],
                                            PROJ[rows, QA, CHUNK * n:CHUNK * n + CHUNK],
                                            kT[rows, CHUNK * n:CHUNK * n + P], start=True, stop=True)
                    ins.then_inc(qk_full, 1)
                    next_group(0, 4, 8)
                    next_group(1)
                    next_group(2, 0, 4)
                    pe.wait_ge(p_ready, it + 1)
                    pe.wait_ge(yh_r, it + 1)
                    pe.wait_ge(vwin_ready, L * 2 + 2)
                    for n in range(8):
                        ins = pe.transpose(bank[6 + n // 4][:, (n % 4) * P:(n % 4) * P + P], Slog[:, n, :], ident[:])
                        if n % 4 == 3:
                            ins.then_inc(pt_full, 1)
                    for c in range(HCHUNKS):
                        ins = pe.transpose(bank[5][:, c * P:c * P + P], PROJ[:, I, c * P:c * P + P], ident[:])
                    ins.then_inc(vtok_full, 1)
                    next_group(2, 4, 5)
                    pe.wait_ge(pt_ready, it * 2 + 2)
                    for n in range(8):
                        for h in range(2):
                            rows = slice(64 * h, 64 * h + 64)
                            ins = pe.matmul(bank[4][rows, CHUNK * n:CHUNK * n + CHUNK], vwin[:, n, rows],
                                            PT[:, n, rows], start=True, stop=True)
                    ins.then_inc(pv_full, 1)
                    pe.wait_ge(staged, it * STAGES + 2)
                    for c in range(HCHUNKS):
                        ins = pe.transpose(bank[6][:, c * P:c * P + P], KH[:, c * P:c * P + P], ident[:])
                    ins.then_inc(kht_full, 1)
                    next_group(2, 5, 6)
                    scores(0)
                    pe.wait_ge(vtok_ready, it + 1)
                    pe.wait_ge(kht_ready, it + 1)
                    for c in range(HCHUNKS - 1):
                        for h in range(2):
                            rows = slice(64 * h, 64 * h + 64)
                            ins = pe.matmul(bank[7][rows, 64 * c:64 * c + 64], KHT[:, c, rows], VTOK[:, c, rows],
                                            start=True, stop=True)
                    ins.then_inc(ds_full, 1)
                    next_group(2, 6, 7)
                    scores(1)
                    next_group(2, 7, 8)
                    scores(2)
                    scores(3)
                    next_group(3, 0, 2)
                    scores(4)
                    next_group(3, 2, 3)
                    scores(5)
                    next_group(3, 3, 5)
                    scores(6)
                    next_group(3, 5, 7)
                    pe.wait_ge(lv_used, (it + 1) * SCORE_SETS)
                    for h in range(2):
                        rows = slice(64 * h, 64 * h + 64)
                        for c in range(HCHUNKS):
                            dst = bank[6][rows, c * P:c * P + P]
                            ins = pe.matmul(dst, VTOK[:, c, rows], SM[:, c, h, :], start=True, stop=(c == 0))
                            if c > 0:
                                ins = pe.matmul(dst, ST[rows, c - 1, :], QB[rows, c * P:c * P + P],
                                                start=False, stop=True)
                    ins.then_inc(o_full, 1)
                    next_group(3, 7, 8)
                    total(YSQ[:], 7, (yh_sq, it + 1), yh_sum, block_ones)
                total(RP[:], 4, (sq_free, L * LAYER_SQ + (Q_YA + NT + SQ_SLOTS)), ya_sum)

                down(L, 1, C_OUT, J_OUT, KT, HHI, HLO, (z_lo, L * 8), k_outer=True)

            pe.wait_ge(const_dma, 16 * 5)
            pe.matmul(bank[0][0:HEADS, 0:RELS], rel_sb, oh_sb, start=True, stop=True).then_inc(setup_pe, 1)
            pe.wait_ge(const_ready, 1)
            with pe.Fori(0, DEPTH) as L:
                ffn(L, 0)
                mixer(L)
                ffn(L, 2)

        @block.vector
        def _(dve):
            def take(L, c, dst, src, i=0, per=0, scale=True, four=None):
                if four is not None and four[1] < 3:
                    dve.wait_ge(four_full, L * 12 + four[0] * 3 + (four[1] + 1))
                else:
                    dve.wait_ge(w_used, L * LAYER_CHUNKS + i * per + (c + 1 + SPLIT_SLOTS))
                if scale:
                    return dve.tensor_tensor(dst, src, R[:], ALU.mult)
                return dve.tensor_copy(dst, src)

            def add_square(L, q, n):
                dve.drain()
                dve.wait_ge(sq_done, L * LAYER_SQ + (q + n + 1))
                sq = SQ[:, (q + n) % 2, :]
                if n == 0:
                    dve.tensor_copy(SS[:], sq).then_inc(sq_free, 1)
                else:
                    dve.tensor_tensor(SS[:], SS[:], sq, ALU.add).then_inc(sq_free, 1)

            def low(L, s, p):
                gain = cur[:, P_GAIN + 2 * s * KT:]
                k, w = INPUT_PARTS[p]
                dve.wait_ge(h_hi, (L * 3 + s) * XT + (p + 1))
                dve.scalar_tensor_tensor(out=HLO[:, k, w], in0=X[:, k, w], scalar=gain[:, k:k + 1],
                                         in1=HHI[:, k, w], op0=ALU.mult, op1=ALU.subtract).then_inc(h_lo, 1)

            def scaled(s, k, w=slice(0, SEQ)):
                gain = cur[:, P_GAIN + (2 * s - 1) * KT:] if s > 0 else out_gain[:]
                dve.scalar_tensor_tensor(out=Y[:, k, w], in0=Y[:, k, w], scalar=gain[:, k:k + 1],
                                         in1=RP[:, w], op0=ALU.mult, op1=ALU.mult)

            def residual(k, w=slice(0, SEQ)):
                dve.tensor_tensor(X[:, k, w], X[:, k, w], Y[:, k, w], ALU.add).then_inc(x_ready, 1)

            def take_last():
                dve.tensor_copy(Y[:, KT - 1, HALVES_OF[1]], bank[6][:, 0:HALF]).then_inc(proj_free, 1)

            def pre(L, s):
                for p, (k, w) in enumerate(INPUT_PARTS):
                    if p == SPLIT_TILES:
                        low(L, s, p - 1)
                    if p % SPLIT_TILES == 0 and p <= SPLIT_TILES:
                        dve.wait_ge(post_r, (L * 3 + s) * 2 + (p // SPLIT_TILES + 1))
                    scaled(s, k, w)
                    dve.drain()
                    if p not in (0, SPLIT_TILES):
                        low(L, s, p - 1)
                    if s == 0 and k % 2 == 0 and p != SPLIT_TILES:
                        dve.wait_ge(x_dma[k // 2], 16)
                    residual(k, w)
                    if k == 3:
                        take_last()
                low(L, s, XT - 1)
                dve.wait_ge(sq_free, L * LAYER_SQ + (Q_PRE[s] + POOL_SQ + SQ_SLOTS))
                dve.sem_inc(held)
                for k in range(POOL_SQ, KT):
                    add_square(L, Q_PRE[s], k)
                dve.wait_ge(pre_r, L * 3 + (s + 1))

            def down(L, s, c0, j0, per, k_outer=False):
                for m in range(KT - 1):
                    c = c0 + 3 if k_outer and m < 4 else c0 + m * per + per - 1
                    take(L, c, Y[:, m, :], bank[m % 4][:], scale=False,
                         four=(2, m) if k_outer and m < 4 else None).then_inc(proj_free, 1)
                    add_square(L, Q_POST[s], m)
                dve.wait_ge(half_sq, L * 3 + (s + 1))
                dve.tensor_copy(Y[:, KT - 1, HALVES_OF[0]], bank[5][:, 0:HALF])

            def ffn(L, s):
                c0, j0, c1, j1 = ((C_UP0, J_UP0, C_DOWN0, J_DOWN0), None, (C_UP1, J_UP1, C_DOWN1, J_DOWN1))[s]
                pre(L, s)

                def body(i, first):
                    for b in range(2):
                        n = (L * 2 + s // 2) * FT + i * 2 + (b + 1)
                        if not (first and b == 0):
                            dve.drain()
                        for g, dst in enumerate((TMP, UB)):
                            j = 2 * b + g
                            take(L, c0 + (3 if first else j), dst[:], bank[j][:], i, 4,
                                 four=(3 * (s // 2), j) if first else None).then_inc(proj_free, 1)
                        dve.drain()
                        dve.wait_ge(silu_ready, n)
                        dve.tensor_tensor(UB[:], UB[:], TMP[:], ALU.mult).then_inc(u_ready, 1)
                        dve.wait_ge(u_hi, n)
                        hi, lo = ((a[:, b, :] if first else a[:, bass.ds(i * 2 + b, 1), :].rearrange("p a n -> p (a n)"))
                                  for a in (UHI, ULO))
                        dve.tensor_tensor(lo, UB[:], hi, ALU.subtract).then_inc(u_lo, 1)
                body(0, True)
                with dve.Fori(1, FT // 2) as i:
                    body(i, False)
                down(L, s, c1, j1, DOWN_CHUNKS)

            def mixer(L):
                pre(L, 1)
                for n, buf in enumerate((kT, vT)):
                    take(L, C_KV + 3, buf[:, CHUNK:], bank[2 + n][:], four=(1, n)).then_inc(proj_free, 1)
                dve.memset(kT[:, 0:CHUNK], 0.0)
                dve.memset(vT[:, 0:CHUNK], 0.0).then_inc(pad_ready, 1)
                for buf in (KZ, QC, SM):
                    dve.memset(buf[:], 0.0)
                dve.memset(RP[:], 0.0)
                chunked = lambda a: a.rearrange("p (c j) -> p c j", c=HCHUNKS)
                dve.wait_ge(setup_dma, 48)
                dve.wait_ge(mask_dma, 16)
                with dve.Fori(0, NT) as t:
                    it = L * NT + t
                    sink = cur[:, bass.ds(t + P_SINK, 1)]
                    lower, upper = lb[:, bass.ds(t, 1)], lb[:, bass.ds(t + NT, 1)]
                    for n in range(4):
                        take(L, C_GROUP0 + n, PROJ[:, n, :], bank[n][:], t, 4).then_inc(proj_free, 1)
                    dve.wait_ge(sig_ready, it + 1)
                    dve.tensor_scalar(SIGF, SIGF, upper, lower, ALU.mult, ALU.add)
                    dve.drain()
                    dve.tensor_scalar(SIGF, SIGF, FG_MIN, None, ALU.max).then_inc(fg_ready, 1)
                    dve.tensor_scalar(KK[:], SIGNF, upper, None, ALU.mult)
                    dve.tensor_tensor(PROJ[:, Q, :], PROJ[:, Q, :], SIGQ, ALU.mult)
                    dve.wait_ge(qk_full, it + 1)
                    bias_t = bias[:, bass.ds(t, 1), :]
                    dve.memset(Slog[:, 0, 0:CHUNK], NEG_INF)
                    for a, z, k0 in ((0, 1, CHUNK), (1, 4, 0), (4, 8, 0)):
                        src = bank[4 + a // 4][:].rearrange("p (n k) -> p n k", n=4)[:, a % 4:a % 4 + z - a, k0:]
                        dve.scalar_tensor_tensor(out=Slog[:, a:z, k0:], in0=src, scalar=HEAD_DIM ** -0.5,
                                                 in1=bias_t[:, :, k0:].to_broadcast([P, z - a, WINDOW - k0]),
                                                 op0=ALU.mult, op1=ALU.add)
                    dve.drain()
                    top = small[:, 0, :]
                    dve.tensor_reduce(top, Slog, AX_X, ALU.max)
                    dve.drain()
                    dve.tensor_scalar(top, top, sink, None, ALU.max)
                    dve.drain()
                    dve.tensor_scalar(Ssink, top, sink, -1.0, ALU.subtract, ALU.mult)
                    dve.tensor_tensor(Slog, Slog, top.unsqueeze(2).to_broadcast([P, 8, WINDOW]), ALU.subtract)\
                        .then_inc(logit_ready, 1)
                    dve.wait_ge(lf_ready, it + 1)
                    for c in range(HCHUNKS):
                        w = slice(c * P, c * P + P)
                        ins = dve.tensor_tensor_scan(BC[:, w], ones[:], LF[:, w], 0.0, ALU.mult, ALU.add)
                    ins.then_inc(bc_ready, 1)
                    dve.wait_ge(exp_ready, it + 1)
                    total, inverse = small[:, 1, :], small[:, 2, :]
                    dve.tensor_reduce(total, Slog, AX_X, ALU.add)
                    dve.drain()
                    dve.tensor_tensor(total, total, Ssink, ALU.add)
                    dve.drain()
                    dve.reciprocal(inverse, total)
                    dve.drain()
                    dve.tensor_tensor(Slog, Slog, inverse.unsqueeze(2).to_broadcast([P, 8, WINDOW]), ALU.mult)\
                        .then_inc(p_ready, 1)

                    def stage(n):
                        dve.wait_ge(decay, it * STAGES + (n + 1))
                        e, q = DD[:, n % DD_SLOTS, :], PROJ[:, Q, :]
                        if n == 0:
                            ins = dve.tensor_tensor(QB[:], q, e, ALU.mult)
                        elif n == 1:
                            ins = dve.tensor_tensor(KH[:], KK[:], e, ALU.mult)
                        elif n == STAGES - 1:
                            dve.sem_inc(held)
                            dve.drain()
                            dve.tensor_tensor(q, q, DD[:, 2, :], ALU.mult)
                            ins = dve.tensor_tensor(KK[:], KK[:], DD[:, 1, :], ALU.mult)
                        else:
                            l, m = n - 2, HALVES[n - 2]
                            halves = lambda a: a.rearrange("p (b u m) -> p b u m", u=2, m=m)
                            for h in range(2):
                                rows = slice(64 * h, 64 * h + 64)
                                cut = lambda a: a[rows].rearrange("p (c b u m) -> p c b u m", c=HCHUNKS, u=2, m=m)[:, :, :, 1, :]
                                packed = QC[rows, l % QC_SLOTS, :, h, :].rearrange("p c (b m) -> p c b m", m=m)
                                dve.tensor_tensor(packed, cut(q), cut(e), ALU.mult)
                            ins = dve.tensor_tensor(halves(KZ[:, l, :])[:, :, 0, :], halves(KK[:])[:, :, 0, :],
                                                    halves(e)[:, :, 0, :], ALU.mult)
                        ins.then_inc(staged, 1)

                    def pick(n):
                        b = 4 + 2 * (n % 2)
                        dve.wait_ge(lv_full, it * SCORE_SETS + (n + 1))
                        dve.sem_inc(held)
                        for l in range(2 * n, min(2 * n + 2, NLEV)):
                            m = HALVES[l]
                            dve.drain()
                            keys = P // 2 if l == 0 else P
                            mask = mask_sb[0:keys, 64 * l:64 * l + 64].rearrange("p (b m) -> p b m", m=m)
                            src = bank[b + l % 2][0:keys, :].rearrange("p (c b m) -> p c b m", c=2 * HCHUNKS, m=m)
                            dst = SM[0:keys].rearrange("p c h (b u m) -> p (c h) b u m", u=2, m=m)[:, :, :, 1, :]
                            ins = dve.copy_predicated(dst, mask.unsqueeze(1).to_broadcast([keys, 2 * HCHUNKS, 64 // m, m]), src)
                        if 2 * n >= NLEV:
                            dve.drain()
                            for h in range(2):
                                ins = dve.copy_predicated(SM[:, :, h, :], pair_sb.unsqueeze(1).to_broadcast([P, HCHUNKS, P]),
                                                          bank[b + h][:].rearrange("p (c j) -> p c j", c=HCHUNKS))
                        ins.then_inc(lv_used, 1)

                    for n in range(5):
                        stage(n)
                    dve.wait_ge(ds_full, it + 1)
                    dve.wait_ge(edec_ready, it + 1)
                    dve.tensor_copy(ST[:, 0, :], bank[7][:, 0:64])
                    for c in range(1, HCHUNKS - 1):
                        dve.drain()
                        ins = dve.scalar_tensor_tensor(out=ST[:, c, :], in0=ST[:, c - 1, :], scalar=edec[:, c:c + 1],
                                                       in1=bank[7][:, 64 * c:64 * c + 64], op0=ALU.mult, op1=ALU.add)
                    ins.then_inc(st_ready, 1)
                    stage(5)
                    pick(0)
                    stage(6)
                    stage(7)
                    stage(8)
                    pick(1)
                    pick(2)
                    pick(3)
                for n in range(NT):
                    take(L, C_GROUPS + 4 * (NT - 1) + n, PROJ[:, n, :], bank[n][:]).then_inc(proj_free, 1)

                def z_low(k):
                    dve.wait_ge(z_hi, L * KT + (k + 1))
                    dve.tensor_tensor(HLO[:, k, :], Y[:, k, :], HHI[:, k, :], ALU.subtract).then_inc(z_lo, 1)
                dve.wait_ge(ya_r, L + 1)
                for k in range(KT):
                    if k < NT:
                        dve.scalar_tensor_tensor(out=Y[:, k, :], in0=Y[:, k, :], scalar=cur[:, P_YA + k:P_YA + k + 1],
                                                 in1=RP[:], op0=ALU.mult, op1=ALU.mult).then_inc(z_ready, 1)
                    else:
                        n = k - NT
                        dve.scalar_tensor_tensor(out=Y[:, k, :], in0=Y[:, k, :], scalar=cur[:, P_YH + n:P_YH + n + 1],
                                                 in1=YR[:, n, :], op0=ALU.mult, op1=ALU.mult)
                        dve.wait_ge(g_sig, L * NT + (n + 1))
                        dve.tensor_tensor(PROJ[:, n, :], PROJ[:, n, :], GATE[:, n, :], ALU.mult)
                        dve.drain()
                        dve.tensor_tensor(Y[:, k, :], Y[:, k, :], PROJ[:, n, :], ALU.mult).then_inc(z_ready, 1)
                    if k > 0:
                        z_low(k - 1)
                z_low(KT - 1)
                down(L, 1, C_OUT, J_OUT, 1, k_outer=True)

            dve.memset(Y[:, 0:KT // 2, :], 0.0)
            dve.memset(RP[:], 0.0)
            dve.memset(bank[6][:, 0:HALF], 0.0)
            dve.memset(out_gain[:], 0.0)
            dve.wait_ge(const_dma, 16 * 5)
            top = lbw[:, 4, :]
            dve.tensor_tensor(top, par[:, 0, P_LB:P_LB + NT], par[:, 1, P_LB:P_LB + NT], ALU.max)
            dve.drain()
            dve.tensor_tensor(lbw[:, 0, :], par[:, 0, P_LB:P_LB + NT], top, ALU.subtract)
            dve.tensor_tensor(lbw[:, 1, :], par[:, 1, P_LB:P_LB + NT], top, ALU.subtract).then_inc(setup, 1)
            dve.wait_ge(setup_pe, 1)
            dve.tensor_copy(rel_rows, bank[0][0:HEADS, 0:RELS]).then_inc(setup, 1)
            dve.wait_ge(setup_act, 1)
            dve.tensor_tensor(lbw[:, 4, :], lbw[:, 2, :], lbw[:, 3, :], ALU.add)
            dve.drain()
            dve.reciprocal(lbw[:, 5, :], lbw[:, 4, :])
            dve.drain()
            dve.tensor_tensor(lbw[:, 0, :], lbw[:, 2, :], lbw[:, 5, :], ALU.mult)
            dve.tensor_tensor(lbw[:, 1, :], lbw[:, 3, :], lbw[:, 5, :], ALU.mult)
            dve.drain()
            dve.tensor_tensor(lb_all[:, 0, 0:NT], lbw[:, 0, :], lbw[:, 0, :], ALU.subtract)
            dve.tensor_tensor(lbw[:, 1, :], lbw[:, 0, :], lbw[:, 1, :], ALU.add)
            dve.drain()
            dve.tensor_tensor(lb_all[:, 1, 0:NT], lbw[:, 1, :], lbw[:, 0, :], ALU.subtract)
            dve.drain()
            dve.tensor_scalar(lb_all[:, :, NT:], lb_all[:, :, 0:NT], -1.0, 1.0, ALU.mult, ALU.add)
            dve.wait_ge(const_ready, 2)
            dve.drain()
            with dve.Fori(0, DEPTH) as L:
                dve.tensor_copy(cur[:], par[:, bass.ds(L, 1), :].rearrange("p a n -> p (a n)"))
                dve.tensor_copy(lb[:], lb_all[:, bass.ds(L, 1), :].rearrange("p a n -> p (a n)"))
                dve.drain()
                for s in (0, 2):
                    g = cur[:, P_GAIN + (2 * s + 1) * KT:P_GAIN + (2 * s + 2) * KT]
                    ins = dve.tensor_scalar(g, g, 0.5, None, ALU.mult)
                ins.then_inc(cur_ready, 1)
                ffn(L, 0)
                mixer(L)
                ffn(L, 2)
                dve.tensor_copy(out_gain[:], cur[:, P_GAIN + 5 * KT:P_GAIN + 6 * KT])
                dve.drain()
            for n, w in enumerate(HALVES_OF):
                dve.wait_ge(post_r, 3 * DEPTH * 2 + n + 1)
                if n == 1:
                    take_last()
                for k in range(SPLIT_TILES):
                    scaled(0, k, w)
                dve.drain()
                for k in range(SPLIT_TILES):
                    residual(k, w)
            for k in LAST_ORDER[SPLIT_TILES:]:
                if k in POOL_TILES:
                    dve.wait_ge(last_scaled, POOL_TILES.index(k) + 1)
                    dve.scalar_tensor_tensor(out=X[:, k, :], in0=Y[:, k, :], scalar=out_gain[:, k:k + 1],
                                             in1=X[:, k, :], op0=ALU.mult, op1=ALU.add).then_inc(x_ready, 1)
                else:
                    scaled(0, k)
                    dve.drain()
                    residual(k)


ACT_WIDTH = HEADS * HEAD_DIM


def weight_stream(w_ffn_in, w_ffn_out, w_in, w_out):
    def columns(w):
        k, n = w.shape[0] // P, w.shape[1] // P
        return w.reshape(k, P, n, P).transpose(2, 1, 0, 3)

    def chunks(tiles, sizes):
        n = tiles.shape[0]
        out = np.zeros((n, len(sizes), P, TILES, P), tiles.dtype)
        at = 0
        for j, size in enumerate(sizes):
            out[:, j, :, :size, :] = tiles[:, :, at:at + size, :]
            at += size
        return out.reshape(n * len(sizes), P, CW)

    def k_outer(tiles):
        return tiles.reshape(4, P, 4, 2, P).transpose(2, 1, 3, 0, 4).reshape(4, P, CW)

    def paired(w, axis):
        order = [t + NT * half for t in range(NT) for half in range(2)]
        shape = w.shape
        w = w.reshape(shape[:axis] + (HEADS, HEAD_DIM) + shape[axis + 1:])
        return np.take(w, order, axis=axis).reshape(shape)

    width, kv = HEADS * HEAD_DIM, 2 * HEAD_DIM
    parts = []
    for layer in range(DEPTH):
        def ffn(j):
            gate_up = columns(w_ffn_in[layer, j])
            order = [n for m in range(FT) for n in (m, FT + m)]
            parts.append(k_outer(gate_up[order[:4]]))
            parts.append(chunks(gate_up[order[4:]], [TILES]))
            sizes = [min(TILES, FT - n * TILES) for n in range(DOWN_CHUNKS)]
            parts.append(chunks(columns(w_ffn_out[layer, j]), sizes))

        ffn(0)
        w = w_in[layer]
        at = 0
        cut = []
        for size in (width, kv, kv, width, width, width, width):
            cut.append(w[:, at:at + size])
            at += size
        qa, ka, va, qh, fh, ih, gh = cut
        group = [columns(a) for a in (fh, paired(qa, 1), qh, ih)]
        parts.append(k_outer(np.stack([group[F][0], group[QA][0], columns(ka)[0], columns(va)[0]])))
        parts.append(chunks(np.stack([group[Q][0], group[I][0]]), [4, 4]))
        parts.append(chunks(np.stack([g[1:] for g in group], axis=1).reshape((-1,) + group[0].shape[1:]), [TILES]))
        parts.append(chunks(columns(gh), [TILES]))
        rows = np.concatenate([paired(w_out[layer, :width], 0), w_out[layer, width:]], axis=0)
        parts.append(k_outer(columns(rows)[:4]))
        parts.append(chunks(columns(rows)[4:], [TILES]))
        ffn(1)
    out = np.concatenate(parts, axis=0)
    assert out.shape == (DEPTH * LAYER_CHUNKS, P, CW)
    return out


def kernel(x, norm_gains, w_ffn_in, w_ffn_out, w_in, w_out, attn_sinks, attn_out_gain,
           rel_bias, hgrn_lb_logits, hgrn_norm_gain):
    import concourse.bacc as bacc
    from concourse.bass_utils import run_bass_kernel_spmd

    def by_partition(a):
        a = np.asarray(a)
        return a.reshape(DEPTH, -1, P).transpose(2, 0, 1)

    ya_gain = np.asarray(attn_out_gain).reshape(DEPTH, 2, NT, HEAD_DIM).transpose(0, 2, 1, 3).reshape(DEPTH, -1)
    params = np.zeros((P, DEPTH, P_SINK), np.float32)
    params[:, :, P_GAIN:P_YA] = by_partition(norm_gains)
    params[:, :, P_YA:P_YH] = by_partition(ya_gain)
    params[:, :, P_YH:P_LB] = by_partition(hgrn_norm_gain)
    params[:, :, P_LB:P_SINK] = by_partition(hgrn_lb_logits)
    arrays = {
        "xT": np.ascontiguousarray(np.asarray(x)[0].reshape(SEQ, KT, P).transpose(2, 1, 0)),
        "stream": weight_stream(*(np.asarray(w) for w in (w_ffn_in, w_ffn_out, w_in, w_out))),
        "params": params,
        "sinks": np.ascontiguousarray(attn_sinks),
        "rel_bias": np.ascontiguousarray(rel_bias),
        "one_hot": t5_bucket_one_hot(),
        "masks": np.concatenate([level_masks(), pair_mask()], axis=1),
    }
    nc = bacc.Bacc("TRN2", target_bir_lowering=False, num_devices=1)
    args = [nc.dram_tensor(n, a.shape, mybir.dt.from_np(a.dtype), kind="ExternalInput").ap() for n, a in arrays.items()]
    out = nc.dram_tensor("yT", (P, KT, SEQ), F32, kind="ExternalOutput").ap()
    build_program(nc, *args, out)
    result = run_bass_kernel_spmd(nc, [arrays], core_ids=[0])
    yT = result.results[0]["yT"]
    return yT.transpose(2, 1, 0).reshape(1, SEQ, D_MODEL)
```
